# Optimizing a Trainium2 kernel written in Bass

```python
import math
import jax, jax.numpy as jnp
from jax import lax
import numpy as np

D_MODEL = 1024
BATCH = 1
SEQ = 256
DEPTH = 4

N_MIXERS = 3
HEAD_DIM = 64
N_HEADS = D_MODEL // HEAD_DIM
MIX_WIDTH = N_HEADS * HEAD_DIM
ROT_DIM = HEAD_DIM // 4
ROPE_THETA = 500000.0
Q_BLOCK = 128
IDX_HEADS = 8
IDX_DIM = 64
IDX_ROT = IDX_DIM // 4
TOPK_MAX = 256
DSA_BLOCK = 32
FOX_HEADS = N_HEADS
MLA_HEADS = N_HEADS
MLA_NOPE = 64
MLA_ROPE = 32
MLA_V = 64
Q_LORA = 384
KV_LORA = 256
D_FF = 2816
ALPHA = (2.0 * DEPTH) ** 0.25
BETA = (8.0 * DEPTH) ** -0.25
LN_EPS = 1e-5
RMS_EPS = 1e-6
N_DSA = (DEPTH + 2) // 3
N_FOX = (DEPTH + 1) // 3
N_MLA = DEPTH // 3
DSA_IN = 3 * MIX_WIDTH + IDX_HEADS * IDX_DIM + IDX_DIM + IDX_HEADS
FOX_IN = 3 * MIX_WIDTH + FOX_HEADS
MLA_IN = Q_LORA + KV_LORA + MLA_ROPE


def layer_norm(x, g, b):
    xf = x.astype(jnp.float32)
    mu = jnp.mean(xf, axis=-1, keepdims=True)
    var = jnp.mean(jnp.square(xf - mu), axis=-1, keepdims=True)
    return ((xf - mu) * lax.rsqrt(var + LN_EPS) * g.astype(jnp.float32) + b.astype(jnp.float32)).astype(x.dtype)

def rms_norm(x, g):
    xf = x.astype(jnp.float32)
    ms = jnp.mean(jnp.square(xf), axis=-1, keepdims=True)
    return (xf * lax.rsqrt(ms + RMS_EPS) * g.astype(jnp.float32)).astype(x.dtype)

def rope_tables(seq_len, dim):
    inv = ROPE_THETA ** (-jnp.arange(0, dim, 2, dtype=jnp.float32) / dim)
    ang = jnp.arange(seq_len, dtype=jnp.float32)[:, None] * inv[None, :]
    return jnp.cos(ang), jnp.sin(ang)

def apply_rope(x, cos, sin):
    half = x.shape[-1] // 2
    x1, x2 = x[..., :half], x[..., half:]
    c = cos[None, :, None, :].astype(x.dtype)
    s = sin[None, :, None, :].astype(x.dtype)
    return jnp.concatenate([x1 * c - x2 * s, x1 * s + x2 * c], axis=-1)

def partial_rope(x, cos, sin, rot):
    return jnp.concatenate([apply_rope(x[..., :rot], cos, sin), x[..., rot:]], axis=-1)

def swiglu(x, w13, w2):
    gate, up = jnp.split(x @ w13, 2, axis=-1)
    return (jax.nn.silu(gate) * up) @ w2

def causal_block_attention(q, k, v, scale, cum=None):
    S = q.shape[1]
    outs = []
    for i in range(S // Q_BLOCK):
        lo, hi = i * Q_BLOCK, (i + 1) * Q_BLOCK
        s = jnp.einsum('bqhd,bkhd->bhqk', q[:, lo:hi], k[:, :hi]).astype(jnp.float32) * scale
        if cum is not None:
            s = s + cum[:, :, lo:hi, None] - cum[:, :, None, :hi]
        mask = jnp.arange(lo, hi)[:, None] >= jnp.arange(hi)[None, :]
        p = jax.nn.softmax(jnp.where(mask, s, -jnp.inf), axis=-1).astype(v.dtype)
        outs.append(jnp.einsum('bhqk,bkhd->bqhd', p, v[:, :hi]))
    return jnp.concatenate(outs, axis=1)

def dsa_mixer(x, w_in, w_out, cos_p, sin_p):
    B, S, _ = x.shape
    d = MIX_WIDTH
    di = IDX_HEADS * IDX_DIM
    q, k, v, qi, ki, wi = jnp.split(x @ w_in, [d, 2 * d, 3 * d, 3 * d + di, 3 * d + di + IDX_DIM], axis=-1)
    q = partial_rope(q.reshape(B, S, N_HEADS, HEAD_DIM), cos_p, sin_p, ROT_DIM)
    k = partial_rope(k.reshape(B, S, N_HEADS, HEAD_DIM), cos_p, sin_p, ROT_DIM)
    v = v.reshape(B, S, N_HEADS, HEAD_DIM)
    qi = partial_rope(qi.reshape(B, S, IDX_HEADS, IDX_DIM), cos_p, sin_p, IDX_ROT)
    ki = partial_rope(ki.reshape(B, S, 1, IDX_DIM), cos_p, sin_p, IDX_ROT)[:, :, 0]
    wi = wi.astype(jnp.float32) * (IDX_HEADS ** -0.5)
    topk = min(TOPK_MAX, S // 4)
    scale = HEAD_DIM ** -0.5
    key_pos = jnp.arange(S)

    def block(i):
        lo = i * DSA_BLOCK
        t = lo + jnp.arange(DSA_BLOCK)
        qb = lax.dynamic_slice_in_dim(q, lo, DSA_BLOCK, axis=1)
        qib = lax.dynamic_slice_in_dim(qi, lo, DSA_BLOCK, axis=1)
        wib = lax.dynamic_slice_in_dim(wi, lo, DSA_BLOCK, axis=1)
        dots = jnp.einsum('bqhd,bkd->bqhk', qib, ki).astype(jnp.float32) * (IDX_DIM ** -0.5)
        idx_score = jnp.einsum('bqh,bqhk->bqk', wib, jax.nn.relu(dots))
        idx_score = jnp.where(t[:, None] >= key_pos[None, :], idx_score, -jnp.inf)
        _, sel = lax.top_k(idx_score, topk)
        ks = jax.vmap(lambda kk, ii: kk[ii])(k, sel)
        vs = jax.vmap(lambda vv, ii: vv[ii])(v, sel)
        logits = jnp.einsum('bqhd,bqkhd->bhqk', qb, ks).astype(jnp.float32) * scale
        valid = sel <= t[None, :, None]
        p = jax.nn.softmax(jnp.where(valid[:, None], logits, -jnp.inf), axis=-1).astype(v.dtype)
        return jnp.einsum('bhqk,bqkhd->bqhd', p, vs)

    out = lax.map(block, jnp.arange(S // DSA_BLOCK))
    out = jnp.transpose(out, (1, 0, 2, 3, 4)).reshape(B, S, d)
    return out @ w_out

def fox_mixer(x, w_in, b_f, w_out):
    B, S, _ = x.shape
    d = MIX_WIDTH
    q, k, v, f = jnp.split(x @ w_in, [d, 2 * d, 3 * d], axis=-1)
    q = q.reshape(B, S, FOX_HEADS, HEAD_DIM)
    k = k.reshape(B, S, FOX_HEADS, HEAD_DIM)
    v = v.reshape(B, S, FOX_HEADS, HEAD_DIM)
    log_f = jax.nn.log_sigmoid(f.astype(jnp.float32) + b_f.astype(jnp.float32))
    cum = jnp.transpose(jnp.cumsum(log_f, axis=1), (0, 2, 1))
    o = causal_block_attention(q, k, v, HEAD_DIM ** -0.5, cum)
    return o.reshape(B, S, d) @ w_out

def mla_mixer(x, w_dqkv, q_norm_g, w_uq, kv_norm_g, w_ukv, w_out, cos_m, sin_m):
    B, S, _ = x.shape
    cq, ckv, k_rope = jnp.split(x @ w_dqkv, [Q_LORA, Q_LORA + KV_LORA], axis=-1)
    q = (rms_norm(cq, q_norm_g) @ w_uq).reshape(B, S, MLA_HEADS, MLA_NOPE + MLA_ROPE)
    q_nope, q_rope = q[..., :MLA_NOPE], apply_rope(q[..., MLA_NOPE:], cos_m, sin_m)
    kv = (rms_norm(ckv, kv_norm_g) @ w_ukv).reshape(B, S, MLA_HEADS, MLA_NOPE + MLA_V)
    k_nope, v = kv[..., :MLA_NOPE], kv[..., MLA_NOPE:]
    k_rope = apply_rope(k_rope[:, :, None, :], cos_m, sin_m)
    q = jnp.concatenate([q_nope, q_rope], axis=-1)
    k = jnp.concatenate([k_nope, jnp.broadcast_to(k_rope, (B, S, MLA_HEADS, MLA_ROPE))], axis=-1)
    o = causal_block_attention(q, k, v, (MLA_NOPE + MLA_ROPE) ** -0.5)
    return o.reshape(B, S, MLA_HEADS * MLA_V) @ w_out

def first_inputs(seed: int = 0) -> dict:
    key = jax.random.key(seed)
    ks = jax.random.split(key, 20)
    nrm = lambda k, shape, fan_in, s=1.0: jax.random.normal(k, shape, jnp.float32) * (fan_in ** -0.5) * s
    x = jax.random.normal(ks[0], (BATCH, SEQ, D_MODEL), jnp.float32)
    ffn1_w13 = nrm(ks[1], (DEPTH, D_MODEL, 2 * D_FF), D_MODEL)
    ffn1_w2 = nrm(ks[2], (DEPTH, D_FF, D_MODEL), D_FF, BETA)
    ffn2_w13 = nrm(ks[3], (DEPTH, D_MODEL, 2 * D_FF), D_MODEL)
    ffn2_w2 = nrm(ks[4], (DEPTH, D_FF, D_MODEL), D_FF, BETA)
    ln_g = 1.0 + 0.02 * jax.random.normal(ks[5], (DEPTH, 3, D_MODEL), jnp.float32)
    ln_b = 0.02 * jax.random.normal(ks[6], (DEPTH, 3, D_MODEL), jnp.float32)
    w_out = nrm(ks[7], (DEPTH, MIX_WIDTH, D_MODEL), MIX_WIDTH, BETA)
    dsa_w_in = nrm(ks[8], (N_DSA, D_MODEL, DSA_IN), D_MODEL)
    fox_w_in = nrm(ks[9], (N_FOX, D_MODEL, FOX_IN), D_MODEL)
    fox_b_f = (jnp.broadcast_to(jnp.linspace(1.0, 6.0, FOX_HEADS, dtype=jnp.float32), (N_FOX, FOX_HEADS))
               + 0.1 * jax.random.normal(ks[10], (N_FOX, FOX_HEADS), jnp.float32))
    mla_w_dqkv = nrm(ks[11], (N_MLA, D_MODEL, MLA_IN), D_MODEL)
    mla_q_norm_g = 1.0 + 0.02 * jax.random.normal(ks[12], (N_MLA, Q_LORA), jnp.float32)
    mla_w_uq = nrm(ks[13], (N_MLA, Q_LORA, MLA_HEADS * (MLA_NOPE + MLA_ROPE)), Q_LORA)
    mla_kv_norm_g = 1.0 + 0.02 * jax.random.normal(ks[14], (N_MLA, KV_LORA), jnp.float32)
    mla_w_ukv = nrm(ks[15], (N_MLA, KV_LORA, MLA_HEADS * (MLA_NOPE + MLA_V)), KV_LORA)
    return {"x": x, "ffn1_w13": ffn1_w13, "ffn1_w2": ffn1_w2, "ffn2_w13": ffn2_w13, "ffn2_w2": ffn2_w2,
            "ln_g": ln_g, "ln_b": ln_b, "w_out": w_out, "dsa_w_in": dsa_w_in, "fox_w_in": fox_w_in,
            "fox_b_f": fox_b_f, "mla_w_dqkv": mla_w_dqkv, "mla_q_norm_g": mla_q_norm_g,
            "mla_w_uq": mla_w_uq, "mla_kv_norm_g": mla_kv_norm_g, "mla_w_ukv": mla_w_ukv}

def first_block(x, ffn1_w13, ffn1_w2, ffn2_w13, ffn2_w2, ln_g, ln_b, w_out, dsa_w_in, fox_w_in,
              fox_b_f, mla_w_dqkv, mla_q_norm_g, mla_w_uq, mla_kv_norm_g, mla_w_ukv):
    S = x.shape[1]
    cos_p, sin_p = rope_tables(S, ROT_DIM)
    cos_m, sin_m = rope_tables(S, MLA_ROPE)
    for i in range(DEPTH):
        x = layer_norm(ALPHA * x + 0.5 * swiglu(x, ffn1_w13[i], ffn1_w2[i]), ln_g[i, 0], ln_b[i, 0])
        kind, j = i % N_MIXERS, i // N_MIXERS
        if kind == 0:
            y = dsa_mixer(x, dsa_w_in[j], w_out[i], cos_p, sin_p)
        elif kind == 1:
            y = fox_mixer(x, fox_w_in[j], fox_b_f[j], w_out[i])
        else:
            y = mla_mixer(x, mla_w_dqkv[j], mla_q_norm_g[j], mla_w_uq[j], mla_kv_norm_g[j],
                          mla_w_ukv[j], w_out[i], cos_m, sin_m)
        x = layer_norm(ALPHA * x + y, ln_g[i, 1], ln_b[i, 1])
        x = layer_norm(ALPHA * x + 0.5 * swiglu(x, ffn2_w13[i], ffn2_w2[i]), ln_g[i, 2], ln_b[i, 2])
    return x


DEPTH_2 = 1

ATTN_SCALE = HEAD_DIM ** -0.5
SWA_HEADS = 8
SWA_KV_HEADS = 2
SWA_WINDOW = 128
SWA_Q = SWA_HEADS * HEAD_DIM
SWA_KV = SWA_KV_HEADS * HEAD_DIM
SSM_WIDTH = 512
SSM_GROUP = 16
SSM_GROUPS = SSM_WIDTH // SSM_GROUP
SSM_STATE = 64
DT_MIN = 0.001
DT_MAX = 0.1
MOBA_HEADS = 8
MOBA_KV_HEADS = 2
MOBA_BLOCK = 256
MOBA_TOPK = 3
MOBA_Q_CHUNK = 64
MOBA_Q = MOBA_HEADS * HEAD_DIM
MOBA_KV = MOBA_KV_HEADS * HEAD_DIM
N_BRANCH = 3
D_FF_2 = 4 * D_MODEL
NORM_EPS = 1e-6
ALIBI_MAX_BIAS = 8.0
IN_SIZES = (SWA_Q, SWA_KV, SWA_KV, SSM_WIDTH, MOBA_Q, MOBA_KV, MOBA_KV, N_BRANCH * D_MODEL)
D_IN = sum(IN_SIZES)


def rms_norm_2(x, gain):
    xf = x.astype(jnp.float32)
    y = xf * lax.rsqrt(jnp.mean(xf * xf, axis=-1, keepdims=True) + NORM_EPS)
    return (y * gain.astype(jnp.float32)).astype(x.dtype)

def alibi_slopes():
    n = SWA_HEADS + MOBA_HEADS
    return jnp.asarray(2.0 ** (-ALIBI_MAX_BIAS * np.arange(1, n + 1) / n), jnp.float32)

def split_in(proj):
    outs, start = [], 0
    for size in IN_SIZES:
        outs.append(proj[..., start:start + size])
        start += size
    return outs

def swa_attention(q, k, v, sinks, slopes):
    B, S, Hq, d = q.shape
    Hkv = k.shape[2]
    G = Hq // Hkv
    W = SWA_WINDOW
    nb = S // W
    qb = q.reshape(B, nb, W, Hkv, G, d)
    kp = jnp.pad(k, ((0, 0), (W, 0), (0, 0), (0, 0))).reshape(B, nb + 1, W, Hkv, d)
    vp = jnp.pad(v, ((0, 0), (W, 0), (0, 0), (0, 0))).reshape(B, nb + 1, W, Hkv, d)
    kb = jnp.concatenate([kp[:, :-1], kp[:, 1:]], axis=2)
    vb = jnp.concatenate([vp[:, :-1], vp[:, 1:]], axis=2)
    s = jnp.einsum('bnqhgd,bnkhd->bnhgqk', qb, kb).astype(jnp.float32) * ATTN_SCALE
    t_rel = jnp.arange(W)[:, None]
    s_rel = jnp.arange(2 * W)[None, :] - W
    dist = t_rel - s_rel
    band = (dist >= 0) & (dist < W)
    mask = band[None] & ((jnp.arange(nb)[:, None, None] * W + s_rel[None]) >= 0)
    bias = -slopes.reshape(Hkv, G)[:, :, None, None] * dist.astype(jnp.float32)[None, None]
    s = jnp.where(mask[None, :, None, None], s + bias[None, None], -jnp.inf)
    sink = jnp.broadcast_to(sinks.astype(jnp.float32).reshape(Hkv, G)[None, None, :, :, None, None],
                            s.shape[:-1] + (1,))
    p = jax.nn.softmax(jnp.concatenate([s, sink], axis=-1), axis=-1)[..., :-1].astype(v.dtype)
    o = jnp.einsum('bnhgqk,bnkhd->bnqhgd', p, vb)
    return o.reshape(B, S, Hq * d)

def moba_attention(q, k, v, slopes):
    B, S, Hq, d = q.shape
    Hkv = k.shape[2]
    G = Hq // Hkv
    L = MOBA_BLOCK
    Qc = MOBA_Q_CHUNK
    Sp = -(-S // L) * L
    nblk = Sp // L
    topk = min(MOBA_TOPK, nblk)
    pad = ((0, 0), (0, Sp - S), (0, 0), (0, 0))
    q, k, v = jnp.pad(q, pad), jnp.pad(k, pad), jnp.pad(v, pad)
    k_blocks = jnp.repeat(k, G, axis=2).transpose(0, 2, 1, 3).reshape(B, Hq, nblk, L, d)
    v_blocks = jnp.repeat(v, G, axis=2).transpose(0, 2, 1, 3).reshape(B, Hq, nblk, L, d)
    k_mean = jnp.mean(k_blocks.astype(jnp.float32), axis=3)
    nq = Sp // Qc
    q_chunks = q.transpose(0, 2, 1, 3).reshape(B, Hq, nq, Qc, d).transpose(2, 0, 1, 3, 4)
    b_idx = jnp.arange(B)[:, None, None, None]
    h_idx = jnp.arange(Hq)[None, :, None, None]
    blk_ids = jnp.arange(nblk)
    rank_ids = jnp.arange(topk)
    offs = jnp.arange(L)

    def one_chunk(args):
        qi, ci = args
        t = ci * Qc + jnp.arange(Qc)
        j = (ci * Qc) // L
        gate = jnp.einsum('bhqd,bhnd->bhqn', qi.astype(jnp.float32), k_mean)
        gate = jnp.where(blk_ids < j, gate, -jnp.inf)
        _, sel = lax.top_k(gate, topk)
        valid = rank_ids < j
        k_sel = k_blocks[b_idx, h_idx, sel]
        v_sel = v_blocks[b_idx, h_idx, sel]
        s_sel = jnp.einsum('bhqd,bhqrkd->bhqrk', qi, k_sel).astype(jnp.float32) * ATTN_SCALE
        dist_sel = (t[None, None, :, None, None] - (sel[..., None] * L + offs)).astype(jnp.float32)
        s_sel = s_sel - slopes[None, :, None, None, None] * dist_sel
        s_sel = jnp.where(valid[None, None, None, :, None], s_sel, -jnp.inf)
        k_own = lax.dynamic_slice_in_dim(k_blocks, j, 1, axis=2)[:, :, 0]
        v_own = lax.dynamic_slice_in_dim(v_blocks, j, 1, axis=2)[:, :, 0]
        s_own = jnp.einsum('bhqd,bhkd->bhqk', qi, k_own).astype(jnp.float32) * ATTN_SCALE
        dist_own = t[:, None] - (j * L + offs)[None, :]
        s_own = s_own - slopes[None, :, None, None] * dist_own.astype(jnp.float32)[None, None]
        s_own = jnp.where((dist_own >= 0)[None, None], s_own, -jnp.inf)
        logits = jnp.concatenate([s_sel.reshape(B, Hq, Qc, topk * L), s_own], axis=-1)
        p = jax.nn.softmax(logits, axis=-1).astype(v_blocks.dtype)
        p_sel = p[..., :topk * L].reshape(B, Hq, Qc, topk, L)
        o = (jnp.einsum('bhqrk,bhqrkd->bhqd', p_sel, v_sel)
             + jnp.einsum('bhqk,bhkd->bhqd', p[..., topk * L:], v_own))
        return o

    o = lax.map(one_chunk, (q_chunks, jnp.arange(nq)))
    o = o.transpose(1, 0, 3, 2, 4).reshape(B, Sp, Hq * d)
    return o[:, :S]

def s5_ssm(u, lam_re, lam_im, log_step, b_re, b_im, c_re, c_im, d_skip):
    Bsz, S, _ = u.shape
    f32 = jnp.float32
    uf = u.astype(f32).reshape(Bsz, S, SSM_GROUPS, SSM_GROUP)
    lr, li = lam_re.astype(f32), lam_im.astype(f32)
    dt = jnp.exp(log_step.astype(f32))[:, None]
    mag = jnp.exp(lr * dt)
    ab_re, ab_im = mag * jnp.cos(li * dt), mag * jnp.sin(li * dt)
    den = lr * lr + li * li
    nr, ni = ab_re - 1.0, ab_im
    f_re, f_im = (nr * lr + ni * li) / den, (ni * lr - nr * li) / den
    br, bi = b_re.astype(f32), b_im.astype(f32)
    bb_re = f_re[..., None] * br - f_im[..., None] * bi
    bb_im = f_re[..., None] * bi + f_im[..., None] * br
    x_re = jnp.einsum('bsgh,gph->bsgp', uf, bb_re)
    x_im = jnp.einsum('bsgh,gph->bsgp', uf, bb_im)
    a_re = jnp.broadcast_to(ab_re, x_re.shape)
    a_im = jnp.broadcast_to(ab_im, x_im.shape)

    def combine(e1, e2):
        a1r, a1i, b1r, b1i = e1
        a2r, a2i, b2r, b2i = e2
        return (a2r * a1r - a2i * a1i, a2r * a1i + a2i * a1r,
                a2r * b1r - a2i * b1i + b2r, a2r * b1i + a2i * b1r + b2i)

    _, _, h_re, h_im = lax.associative_scan(combine, (a_re, a_im, x_re, x_im), axis=1)
    y = (jnp.einsum('bsgp,ghp->bsgh', h_re, c_re.astype(f32))
         - jnp.einsum('bsgp,ghp->bsgh', h_im, c_im.astype(f32))
         + d_skip.astype(f32).reshape(SSM_GROUPS, SSM_GROUP) * uf)
    return y.reshape(Bsz, S, SSM_WIDTH)

def second_inputs(seed: int = 0) -> dict:
    key = jax.random.key(seed)
    ks = jax.random.split(key, 24)
    f32 = jnp.float32
    nrm = lambda k, shape, scale: jax.random.normal(k, shape, f32) * scale
    x = jax.random.normal(ks[0], (BATCH, SEQ, D_MODEL), f32)
    norm_mix = 1.0 + nrm(ks[1], (DEPTH_2, D_MODEL), 0.02)
    w_in = nrm(ks[2], (DEPTH_2, D_MODEL, D_IN), D_MODEL ** -0.5)
    sinks = nrm(ks[3], (DEPTH_2, SWA_HEADS), 0.5)
    lam_re = -0.5 + nrm(ks[4], (DEPTH_2, SSM_GROUPS, SSM_STATE), 0.01)
    lam_im = (math.pi * jnp.arange(SSM_STATE, dtype=f32))[None, None, :] + nrm(ks[5], (DEPTH_2, SSM_GROUPS, SSM_STATE), 0.01)
    log_step = math.log(DT_MIN) + jax.random.uniform(ks[6], (DEPTH_2, SSM_GROUPS), f32) * (math.log(DT_MAX) - math.log(DT_MIN))
    b_re = nrm(ks[7], (DEPTH_2, SSM_GROUPS, SSM_STATE, SSM_GROUP), (2 * SSM_GROUP) ** -0.5)
    b_im = nrm(ks[8], (DEPTH_2, SSM_GROUPS, SSM_STATE, SSM_GROUP), (2 * SSM_GROUP) ** -0.5)
    c_re = nrm(ks[9], (DEPTH_2, SSM_GROUPS, SSM_GROUP, SSM_STATE), (2 * SSM_STATE) ** -0.5)
    c_im = nrm(ks[10], (DEPTH_2, SSM_GROUPS, SSM_GROUP, SSM_STATE), (2 * SSM_STATE) ** -0.5)
    d_skip = nrm(ks[11], (DEPTH_2, SSM_WIDTH), 1.0)
    w_glu = nrm(ks[12], (DEPTH_2, SSM_WIDTH, 2 * SSM_WIDTH), SSM_WIDTH ** -0.5)
    w_o_swa = nrm(ks[13], (DEPTH_2, SWA_Q, D_MODEL), SWA_Q ** -0.5)
    w_o_ssm = nrm(ks[14], (DEPTH_2, SSM_WIDTH, D_MODEL), SSM_WIDTH ** -0.5)
    w_o_moba = nrm(ks[15], (DEPTH_2, MOBA_Q, D_MODEL), MOBA_Q ** -0.5)
    w_out = nrm(ks[16], (DEPTH_2, D_MODEL, D_MODEL), D_MODEL ** -0.5)
    norm_ffn = 1.0 + nrm(ks[17], (DEPTH_2, D_MODEL), 0.02)
    w_ff1 = nrm(ks[18], (DEPTH_2, D_MODEL, D_FF_2), D_MODEL ** -0.5)
    w_ff2 = nrm(ks[19], (DEPTH_2, D_FF_2, D_MODEL), D_FF_2 ** -0.5)
    norm_final = 1.0 + nrm(ks[20], (D_MODEL,), 0.02)
    return {"x": x, "norm_mix": norm_mix, "w_in": w_in, "sinks": sinks,
            "lam_re": lam_re, "lam_im": lam_im, "log_step": log_step,
            "b_re": b_re, "b_im": b_im, "c_re": c_re, "c_im": c_im, "d_skip": d_skip,
            "w_glu": w_glu, "w_o_swa": w_o_swa, "w_o_ssm": w_o_ssm, "w_o_moba": w_o_moba,
            "w_out": w_out, "norm_ffn": norm_ffn, "w_ff1": w_ff1, "w_ff2": w_ff2,
            "norm_final": norm_final}

def second_block(x, norm_mix, w_in, sinks, lam_re, lam_im, log_step, b_re, b_im, c_re, c_im,
              d_skip, w_glu, w_o_swa, w_o_ssm, w_o_moba, w_out, norm_ffn, w_ff1, w_ff2,
              norm_final):
    B, S, _ = x.shape
    slopes = alibi_slopes()
    slopes_swa, slopes_moba = slopes[:SWA_HEADS], slopes[SWA_HEADS:]
    for l in range(DEPTH_2):
        h = rms_norm_2(x, norm_mix[l])
        qa, ka, va, u, qm, km, vm, gates = split_in(h @ w_in[l])
        oa = swa_attention(qa.reshape(B, S, SWA_HEADS, HEAD_DIM),
                           ka.reshape(B, S, SWA_KV_HEADS, HEAD_DIM),
                           va.reshape(B, S, SWA_KV_HEADS, HEAD_DIM), sinks[l], slopes_swa)
        ya = oa @ w_o_swa[l]
        ys = s5_ssm(u, lam_re[l], lam_im[l], log_step[l], b_re[l], b_im[l], c_re[l], c_im[l], d_skip[l])
        z = jax.nn.gelu(ys).astype(x.dtype) @ w_glu[l]
        yb = (z[..., :SSM_WIDTH] * jax.nn.sigmoid(z[..., SSM_WIDTH:])) @ w_o_ssm[l]
        om = moba_attention(qm.reshape(B, S, MOBA_HEADS, HEAD_DIM),
                            km.reshape(B, S, MOBA_KV_HEADS, HEAD_DIM),
                            vm.reshape(B, S, MOBA_KV_HEADS, HEAD_DIM), slopes_moba)
        yc = om @ w_o_moba[l]
        g = jax.nn.sigmoid(gates)
        mixed = (g[..., :D_MODEL] * ya + g[..., D_MODEL:2 * D_MODEL] * yb
                 + g[..., 2 * D_MODEL:] * yc)
        x = x + mixed @ w_out[l]
        h = rms_norm_2(x, norm_ffn[l])
        x = x + jnp.square(jax.nn.relu(h @ w_ff1[l])) @ w_ff2[l]
    return rms_norm_2(x, norm_final)


def setup_inputs(seed=0):
    out = dict(first_inputs(seed))
    for name, value in second_inputs(seed + 1).items():
        if name != "x":
            out[name + "_2"] = value
    return out


def reference(
    x, ffn1_w13, ffn1_w2, ffn2_w13, ffn2_w2, ln_g, ln_b, w_out, dsa_w_in, fox_w_in, fox_b_f,
    mla_w_dqkv, mla_q_norm_g, mla_w_uq, mla_kv_norm_g, mla_w_ukv, norm_mix_2, w_in_2, sinks_2,
    lam_re_2, lam_im_2, log_step_2, b_re_2, b_im_2, c_re_2, c_im_2, d_skip_2, w_glu_2,
    w_o_swa_2, w_o_ssm_2, w_o_moba_2, w_out_2, norm_ffn_2, w_ff1_2, w_ff2_2, norm_final_2,
):
    x = first_block(
        x, ffn1_w13, ffn1_w2, ffn2_w13, ffn2_w2, ln_g, ln_b, w_out, dsa_w_in, fox_w_in, fox_b_f,
        mla_w_dqkv, mla_q_norm_g, mla_w_uq, mla_kv_norm_g, mla_w_ukv,
    )
    return second_block(
        x, norm_mix_2, w_in_2, sinks_2, lam_re_2, lam_im_2, log_step_2, b_re_2, b_im_2, c_re_2,
        c_im_2, d_skip_2, w_glu_2, w_o_swa_2, w_o_ssm_2, w_o_moba_2, w_out_2, norm_ffn_2,
        w_ff1_2, w_ff2_2, norm_final_2,
    )


_drawn_inputs = setup_inputs


def setup_inputs(seed=0):
    import zlib

    import numpy as np

    out = dict(_drawn_inputs(seed))
    spreads = {}
    factors = {'mla_q_norm_g': 8.0,
     'mla_kv_norm_g': 8.0,
     'norm_mix_2': 5.933,
     'sinks_2': 44.072,
     'lam_re_2': 64.0,
     'lam_im_2': 37.856,
     'log_step_2': 39.736,
     'b_re_2': 54.056,
     'b_im_2': 53.712,
     'c_re_2': 54.224,
     'c_im_2': 53.064,
     'norm_ffn_2': 8.699,
     'norm_final_2': 7.992}
    for name, (base, spread) in spreads.items():
        noise = np.random.default_rng([zlib.crc32(name.encode()), seed]).standard_normal(out[name].shape)
        drawn = base * np.exp(spread * noise) if base else spread * noise
        out[name] = __import__('jax').numpy.asarray(drawn.astype(out[name].dtype))
    for name, factor in factors.items():
        out[name] = (out[name] * factor).astype(out[name].dtype)
    return out
```

```python
from contextlib import ExitStack

import numpy as np

import concourse.bass as bass
from concourse import mybir

F32 = mybir.dt.float32
F32R = mybir.dt.float32r
ALU = mybir.AluOpType
ACT = mybir.ActivationFunctionType
AX_X = mybir.AxisListType.X

P = 128
S = 256
NT = S // P
DM = 1024
KT = DM // P
DEPTH = 4
NH = 16
DH = 64
DFF = 2816
FIT = DFF // 256
DFF2 = 4096
QL, KVL, RP = 384, 256, 32
MD = DH + RP
SLOTS = 3
W = 2048
NG = 4
ALPHA = (2.0 * DEPTH) ** 0.25
LN_EPS, RMS_EPS = 1e-5, 1e-6
NEG = -1e30
TAKEN = -(2.0 ** 127)
TOPK = S // 4
MLA_IN = QL + KVL + RP
SS = 512
FK = DFF2 // 256
NQ2 = 2
INV2PI = 1.0 / (2.0 * np.pi)
ROUND = 1.5 * 2.0 ** 23
PI1 = 6.28125
PI2 = float((np.array([2 * np.pi - PI1], np.float32).view(np.uint32) & np.uint32(0xFFFFF000)).view(np.float32)[0])
PI3 = float(np.float32(2 * np.pi - PI1 - PI2))
PI_IN = 3.1415925


def tables():
    q = np.arange(P)[:, None]
    ident = np.eye(P, dtype=np.float32)
    dist = np.concatenate([q - np.arange(P)[None], P + q - np.arange(S)[None]], 1).astype(np.float32)
    causal = np.where(dist >= 0, 0.0, NEG).astype(np.float32)
    window = np.where((dist >= 0) & (dist < 128), 0.0, NEG).astype(np.float32)

    def rope(dim):
        inv = np.float32(500000.0) ** (-np.arange(0, dim, 2, dtype=np.float32) / np.float32(dim))
        ang = np.arange(S, dtype=np.float32)[:, None] * inv[None].astype(np.float32)
        cs = np.stack([np.cos(ang), np.sin(ang)], 1).astype(np.float32)
        return cs.reshape(NT, P, 2, dim // 2).transpose(1, 2, 0, 3)

    rp, rm = rope(16), rope(RP)
    rp2 = np.concatenate([rp, rp], 2)
    upper = (np.arange(S)[:, None] <= np.arange(S)[None]).astype(np.float32) * np.float32(-8.0)
    upper = upper.reshape(NT, P, S).transpose(1, 0, 2)
    return {
        "ident": ident, "causal": causal, "window": window, "dist": dist,
        "ramp": np.broadcast_to(np.arange(S, dtype=np.float32), (P, S)),
        "rope_p": rp2.reshape(P, -1), "rope_m": rm.reshape(P, -1), "upper": upper.reshape(P, -1),
    }


MADE = {
    "init": dict(t_done=4, xt_dve=4, xt_act=4, xh_ready=4, xl_ready=4, cx_ready=4),
    "norm": dict(var_ready=2, rstd_ready=2, nmr_ready=2, xn_act=2, xn_dve=2, t_done=4, xt_dve=4,
                 xt_act=4, xh_ready=4, xl_ready=4, cx_ready=4),
    "ffn": dict(silu_done=FIT, up0_done=FIT, g_made=2 * FIT, gh_ready=2 * FIT, gl_ready=2 * FIT),
    "attn": dict(v_moved=NG, s_filled=NH, masked=NH, nb_ready=NH, exp_done=NH,
                 rs_ready=NH, p_ready=NH, av_done=NH, oh_ready=NH // 2, ol_ready=NH // 2),
    "final": dict(var_ready=2, rstd_ready=2, nmr_ready=2, xn_act=2, xn_dve=2),
    "index": dict(rope_done=2),
    "latent": dict(rope_done=1),
    "oproj": {},
}


CREDITS = {
    "tensor": dict(x_filled=2, av_done=1),
    "vector": dict(masked=2, ol_ready=1, v_moved=1, x_moved0=1),
    "scalar": dict(exp_done=2, x_moved1=1),
    "gpsimd": dict(p_ready=2, rope_done=1),
}


def stages_plan(upto=99):
    plan = [dict(kind="init", c=2 * ALPHA)]
    for layer in range(DEPTH):
        mix = ("dsa", "fox", "mla", "dsa")[layer]
        plan.append(dict(kind="ffn", w=0, layer=layer, units=3 * FIT))
        plan.append(dict(kind="norm", g=3 * layer, eps=4 * LN_EPS, c=ALPHA))
        if mix == "dsa":
            plan.append(dict(kind="index", layer=layer, j=layer // 3, units=3))
        if mix == "fox":
            plan.append(dict(kind="forget", layer=layer, units=1))
        if mix == "mla":
            plan.append(dict(kind="latent", layer=layer, units=3))
        plan.append(dict(kind="attn", mix=mix, layer=layer, j=layer // 3, units=3 * NG))
        plan.append(dict(kind="oproj", layer=layer, units=4))
        plan.append(dict(kind="norm", g=3 * layer + 1, eps=LN_EPS, c=2 * ALPHA))
        plan.append(dict(kind="ffn", w=1, layer=layer, units=3 * FIT))
        plan.append(dict(kind="norm", g=3 * layer + 2, eps=4 * LN_EPS,
                         c=2 * ALPHA if layer < DEPTH - 1 else 1.0))
    plan += [
        dict(kind="lift"),
        dict(kind="norm", g=12, eps=RMS_EPS, rms=True),
        dict(kind="attn", mix="swa", units=3, col=0, out=0),
        dict(kind="attn", mix="moba", units=3, col=1280, out=4),
        dict(kind="ssm_in", units=2),
        dict(kind="ssm"),
        dict(kind="glu", units=2),
        dict(kind="branches", units=18),
        dict(kind="oproj2", units=4),
        dict(kind="norm", g=13, eps=RMS_EPS, rms=True, keep=True),
        dict(kind="ff", units=2 * FK),
        dict(kind="final", eps=RMS_EPS, rms=True),
    ]
    unit, base = 0, {name: n for names in CREDITS.values() for name, n in names.items()}
    for st in plan:
        st.setdefault("units", 0)
        st["u"] = unit
        st["base"] = dict(base)
        unit += st["units"]
        made = dict(MADE.get(st["kind"], {}))
        if st["kind"] == "norm" and "rms" in st:
            made.pop("cx_ready")
        if st["kind"] == "attn" and st["mix"] in ("swa", "moba"):
            made = {k: n // 2 for k, n in made.items()}
            made.update(v_moved=1, qk_moved=4, x_filled=12, x_moved0=6, x_moved1=6)
        elif st["kind"] == "attn":
            rounds = 8 if st["mix"] == "mla" else 6
            made.update(qk_moved=(3 if st["mix"] == "mla" else 2) * NG, x_filled=rounds * NG, x_moved0=rounds // 2 * NG, x_moved1=rounds // 2 * NG)
            if st["mix"] == "mla":
                made["v_moved"] = 0
            if st["mix"] != "fox":
                made["rope_done"] = NG
        for k, n in made.items():
            base[k] = base.get(k, 0) + n
        st["end"] = unit
    return plan, unit


(LS, DT, LR, LI, AL, RHO, PH, PHR, PHH, PHL, SI, CO, NR, NI, DEN, FR, FI, T0, T1, T2) = range(20)


class Chain:

    def __init__(self, eng, sem):
        self.eng, self.sem, self.n = eng, sem, 0

    def link(self, ins):
        ins.then_inc(self.sem, 1)
        self.n += 1

    def wait(self):
        self.eng.wait_ge(self.sem, self.n)

    def step(self, ins):
        self.link(ins)
        self.wait()


def build(nc, a, out, plan, n_units):
    T = tables()
    with ExitStack() as ctx:
        def sb(name, shape, dt=F32):
            return ctx.enter_context(nc.sbuf_tensor(name, shape, dt))

        sems = {}

        def sem(name):
            if name not in sems:
                sems[name] = ctx.enter_context(nc.semaphore(name))
            return sems[name]

        raw = sb("raw", [P, SLOTS, W])
        whi = sb("whi", [P, SLOTS, W], F32R)
        wlo = sb("wlo", [P, SLOTS, W], F32R)
        xT = sb("xT", [P, KT, S])
        xh = sb("xh", [P, KT, S], F32R)
        xl = sb("xl", [P, KT, S], F32R)
        cx = sb("cx", [P, KT, S])
        oh = sb("oh", [P, KT, S], F32R)
        ol = sb("ol", [P, KT, S], F32R)
        xn = sb("xn", [P, NT, DM])
        sg = sb("sg", [P, 2, S])
        gt = sb("gt", [P, 2, S])
        qk_tm = sb("qk_tm", [P, 2 * NT * 4 * MD])
        v_tm = sb("v_tm", [P, NT, 4, DH])
        qkT = sb("qkT", [P, 4, 4 * P])
        s_sb = sb("s_sb", [P, 2, 3 * P])
        pr = sb("pr", [P, 2, 3 * P])
        pT = sb("pT", [P, 2, 3 * P])
        mx = sb("mx", [P, 2, 2])
        nb = sb("nb", [P, 2, 2])
        sm = sb("sm", [P, 2, 2])
        rs = sb("rs", [P, 2, 2])
        rt = sb("rt", [P, 4, 4 * 4 * 8])
        selcum_all = sb("selcum", [P, NH * S])
        selcum = selcum_all[0:16, :].rearrange("p (h s) -> p h s", h=NH)
        bias = sb("bias", [P, 3 * P])
        acc = sb("acc", [P, 3 * P])
        ident = sb("ident", [P, P])
        masks = sb("masks", [P, 3, 3 * P])
        causal = masks[:, 0, :]
        distp = masks[:, 1, :]
        windowp = masks[:, 2, :]
        rope_p = sb("rope_p", [P, 2, 4, 8])
        rope_m = sb("rope_m", [P, 2, NT, RP // 2])
        upper = sb("upper", [P, NT, S])
        gains = sb("gains", [P, P])
        shifts = sb("shifts", [P, P])
        fb = sb("fb", [P, NH])
        ones = sb("ones", [P, P])
        mhalf = sb("mhalf", [P, 2])
        halfpi = sb("halfpi", [P, 1])
        st6 = sb("st6", [P, NT, 2, 6])
        mv = sb("mv", [P, NT, 2])
        ve = sb("ve", [P, NT, 2])
        rstd = sb("rstd", [P, NT, 2])
        nmr = sb("nmr", [P, NT])
        wi = sb("wi", [P, NT, 8])
        m8 = sb("m8", [P, 2, 8])
        bh = sb("bh", [P, 4, S], F32R)
        bl = sb("bl", [P, 4, S], F32R)
        ramp = sb("ramp", [P, S])
        snk = sb("snk", [P, 2, 8])
        esk = sb("esk", [P, 2, 2])
        cc = sb("cc", [P, 4, 2, 64])
        bb = sb("bb", [P, 2, 16, 16])
        BT = sb("BT", [P, 8, P])
        prm = sb("prm", [P, 20, 16])
        tick = sb("tick", [P, 1])
        kr = sb("kr", [P, NT, RP])
        v_nx = sg[:, :, :].rearrange("p t (h d) -> p t h d", h=4)
        zf = gt[:, 0, 0:3 * NT * NH].rearrange("p (n t h) -> p n t h", n=3, t=NT)
        m8z = gt[:, 1, 0:3 * NT * NH].rearrange("p (n t h) -> p n t h", n=3, t=NT)

        ps = ctx.enter_context(nc.psum_tensor("ps", [P, 8, 512], F32))
        y = ps[:, 0:4, :].rearrange("p (t n) c -> p t n c", t=NT)
        tb = ps[:, 4:8, :].rearrange("p b (k s) -> p (b k) s", k=2)

        G = {"qn": 112, "kvn": 115}

        def s_flat(t):
            return t[:, :, :].rearrange("p a b -> p (a b)")[:, 0:512].rearrange("p (r s) -> p r s", r=2)

        def bc(ap, axis, shape):
            return ap.unsqueeze(axis).broadcast_to(shape)

        def split_units(st):
            return [u + SLOTS for u in range(st["u"], st["end"]) if u + SLOTS < n_units]

        N_CONSTS = 24 * 16

        kd = qk_tm[:, 1024:1536].rearrange("p (t g n d) -> p t g n d", t=NT, g=2, n=2)
        flat = qkT[:, :, :].rearrange("p a c -> p (a c)")
        grow, brow = flat[:, 0:P], flat[:, P:2 * P]
        ls16 = flat[0:16, 2 * P:3 * P].rearrange("p (g d) -> p g d", g=2)
        ls2 = flat[0:16, 3 * P:3 * P + 2]
        Z = flat[:, 0:1024].rearrange("p (j r c) -> p j r c", j=4, r=2)
        CL = flat[:, 1024:2048].rearrange("p (j r c) -> p j r c", j=4, r=2)
        sinT = selcum_all[:, :].rearrange("p (j s) -> p j s", j=16)
        uT = qk_tm[:, 0:1024].rearrange("p (q s) -> p q s", q=4)
        ysT = qk_tm[:, 1024:1536].rearrange("p (q s) -> p q s", q=2)
        ta, tb2 = sg, gt
        wv = v_tm[:, :, :, :].rearrange("p t h d -> p t (h d)")
        pa = masks[:, 1:3, :].rearrange("p a b -> p (a b)")[:, 0:2 * S].rearrange("p (t s) -> p t s", t=2)
        pb = rt[:, :, :].rearrange("p (a b) c -> p a (b c)", a=2)
        gv = [s_flat(s_sb), s_flat(pr)]
        hv = [s_flat(pT), upper]
        x2 = cx[:, :, :].rearrange("p (t k) s -> p t (k s)", t=NT)
        brr = s_sb[:, :, :].rearrange("p a b -> p (a b)")[:, 0:512].rearrange("p (r j h) -> p r j h", r=2, j=16)

        def cosT(j):
            o = (xn[:, :, :].rearrange("p t c -> p (t c)") if j < 8 else xT[:, :, :].rearrange("p k s -> p (k s)"))
            return o[:, (j % 8) * S:(j % 8 + 1) * S]

        def load(sp, u, u0, src, width):
            slot = u0 % SLOTS
            if u0 >= SLOTS:
                sp.wait_ge(sem("lo_ready"), u - SLOTS + 1)
            dst = raw[:, slot, 0:width]
            if len(src.shape) == 3:
                dst = dst.rearrange("p (k c) -> p k c", k=src.shape[1])
            sp.dma_start(dst, src).then_inc(sem(f"loaded{slot}"), 16)

        def split_hi(act, du, u0):
            if u0 >= n_units:
                return
            slot = u0 % SLOTS
            w = widths[u0] if isinstance(du, int) else W
            if isinstance(du, int):
                act.wait_ge(sem(f"loaded{slot}"), 16 * ((u0 + du) // SLOTS + 1))
            else:
                i, per = du
                act.wait_ge(sem(f"loaded{slot}"), i * (16 * per // SLOTS) + 16 * (u0 // SLOTS + 1))
            if u0 >= SLOTS:
                act.wait_ge(sem("unit_used"), at(du, u0 - SLOTS + 1))
            act.activation(whi[:, slot, 0:w], raw[:, slot, 0:w], ACT.Copy).then_inc(sem("hi_ready"), 1)

        def split_lo(dve, du, u0):
            if u0 >= n_units:
                return
            slot = u0 % SLOTS
            w = widths[u0] if isinstance(du, int) else W
            dve.wait_ge(sem("hi_ready"), at(du, u0 + 1))
            dve.tensor_tensor(wlo[:, slot, 0:w], raw[:, slot, 0:w], whi[:, slot, 0:w].bitcast(F32),
                              ALU.subtract).then_inc(sem("lo_ready"), 1)

        def at(du, u0):
            return u0 + du if isinstance(du, int) else du[0] * du[1] + u0

        def unit_ready(pe, du, u0):
            pe.wait_ge(sem("lo_ready"), at(du, u0 + 1))

        rows = "(k p) n -> p k n"

        def sources(st, i):
            kind, L = st["kind"], st.get("layer")
            if kind == "ffn":
                w13 = a["ffn1_w13" if st["w"] == 0 else "ffn2_w13"][L].rearrange(rows, p=P)
                w2 = a["ffn1_w2" if st["w"] == 0 else "ffn2_w2"][L].rearrange(rows, p=P)
                return [w13[:, :, bass.ds(256 * i, 256)], w13[:, :, bass.ds(DFF + 256 * i, 256)],
                        w2[:, bass.ds(2 * i, 2), :]]
            if kind == "index":
                w = a["dsa_w_in"][st["j"]].rearrange(rows, p=P)
                return [w[:, :, 3072:3328], w[:, :, 3328:3584], w[:, :, 3584:3656]]
            if kind == "forget":
                return [a["fox_w_in"][0].rearrange(rows, p=P)[:, :, 3072:3088]]
            if kind == "latent":
                w = a["mla_w_dqkv"][0].rearrange(rows, p=P)
                return [w[:, 0:3, :], w[:, 3:6, :], w[:, 6:8, :]]
            if kind == "attn" and st["mix"] == "mla":
                uq = a["mla_w_uq"][0].rearrange(rows, p=P)
                ukv = a["mla_w_ukv"][0].rearrange(rows, p=P)
                return [uq[:, :, bass.ds(384 * i, 384)], ukv[:, :, bass.ds(512 * i, 256)],
                        ukv[:, :, bass.ds(512 * i + 256, 256)]]
            if kind == "attn" and "col" not in st:
                w = a["dsa_w_in"][st["j"]] if st["mix"] == "dsa" else a["fox_w_in"][0]
                w = w.rearrange(rows, p=P)
                return [w[:, :, bass.ds(1024 * m + 256 * i, 256)] for m in range(3)]
            if kind == "oproj":
                w = a["w_out"][L].rearrange(rows, p=P)
                return [w[:, 2 * m:2 * m + 2, :] for m in range(4)]
            if kind == "ssm_in" or (kind == "attn" and "col" in st):
                w = a["w_in_2"][0].rearrange(rows, p=P)
                c = st.get("col", 768)
                return [w[:, :, c + 256 * m:c + 256 * m + 256] for m in range(st["units"])]
            if kind == "glu":
                w = a["w_glu_2"][0].rearrange(rows, p=P)
                return [w[:, :, 512 * m:512 * m + 512] for m in range(2)]
            if kind == "branches":
                w = a["w_in_2"][0].rearrange(rows, p=P)
                out_ = []
                for J in range(2):
                    for name in ("w_o_swa_2", "w_o_ssm_2", "w_o_moba_2"):
                        out_.append(a[name][0].rearrange(rows, p=P)[:, :, 512 * J:512 * J + 512])
                    for jj in range(2):
                        for m in range(3):
                            c = 2048 + DM * m + 512 * J + 256 * jj
                            out_.append(w[:, :, c:c + 256])
                return out_
            if kind == "oproj2":
                w = a["w_out_2"][0].rearrange(rows, p=P)
                return [w[:, 2 * m:2 * m + 2, :] for m in range(4)]
            return []

        widths = []
        for st in plan:
            per = [int(np.prod(s.shape[1:])) for s in sources(st, 0)] if st["kind"] != "ff" else [W]
            widths += per * (st["units"] // len(per)) if per else []
        assert len(widths) == n_units

        def mm3(pe, o, ah, al, bh, bl, start, stop):
            pe.matmul(o, ah, bh, start=start, stop=False, skip_group_check=True)
            pe.matmul(o, ah, bl, start=False, stop=False, skip_group_check=True)
            return pe.matmul(o, al, bh, start=False, stop=stop, skip_group_check=True)

        def feature_major(pe, o, slot, c0, kts, width, h=None, l=None, lows=None):
            h, l = (xh, xl) if h is None else (h, l)
            for k in range(kts):
                if lows is not None and k % 2 == 0:
                    pe.wait_ge(sem("xl_ready"), lows + k // 2 + 1)
                c = k * width + c0
                last = mm3(pe, o, whi[:, slot, c:c + P], wlo[:, slot, c:c + P], h[:, k, :],
                           l[:, k, :], k == 0, k == kts - 1)
            return last

        def token_major(pe, o, slot, c0, n, t, ks, width, k0=0, first=True, final=True, src=(xh, xl),
                        row0=0):
            for k in ks:
                c = (k - row0) * width + c0
                last = mm3(pe, o, src[0][:, k0 + k, t * P:(t + 1) * P],
                           src[1][:, k0 + k, t * P:(t + 1) * P], whi[:, slot, c:c + n],
                           wlo[:, slot, c:c + n], first and k == ks[0], final and k == ks[-1])
            return last

        def down(pe, slot, src, k0, final, order=((0, 0), (0, 1), (1, 0), (1, 1))):
            for t, n in order:
                last = mm3(pe, y[:, t, n, :], src[0][:, k0, t * P:(t + 1) * P],
                           src[1][:, k0, t * P:(t + 1) * P],
                           whi[:, slot, n * 512:n * 512 + 512], wlo[:, slot, n * 512:n * 512 + 512],
                           False, final)
            return last

        def residual(pe, st):
            pe.wait_ge(sem("cx_ready"), st["base"]["cx_ready"])
            for t in range(NT):
                for k in range(KT):
                    pe.matmul(y[:, t, k // 4, (k % 4) * P:(k % 4 + 1) * P],
                              cx[:, k, t * P:(t + 1) * P], ident[:, :], is_transpose=True,
                              start=k % 4 == 0, stop=False, skip_group_check=True)

        block = ctx.enter_context(nc.Block())

        @block.sync
        def _(sp):
            consts = [(ident, "ident"), (causal, "causal"), (rope_p, "rope_p"), (rope_m, "rope_m"),
                      (upper, "upper"), (ramp, "ramp"), (distp, "dist"), (windowp, "window")]
            x_rows = a["x"][0].rearrange("(t p) n -> p t n", p=P)
            sp.dma_start(xn[:, :, :], x_rows).then_inc(sem("x_loaded"), 16)
            for j, src in enumerate(sources(plan[1], 0)):
                load(sp, j, j, src, widths[j])
            for n, (dst, name) in enumerate(consts):
                src = nc.inline_tensor(np.ascontiguousarray(T[name]), name=name + "_table").ap()
                d = dst[:, :] if len(dst.shape) == 2 else (
                    dst[:, :, :].rearrange("p a b -> p (a b)") if len(dst.shape) == 3 else
                    dst[:, :, :, :].rearrange("p a b c -> p (a b c)"))
                sp.dma_start(d, src).then_inc(sem("consts"), 16)
            sp.dma_start(grow[0:96, :], a["ln_g"].rearrange("l m (k p) -> (l m k) p", p=P)).then_inc(sem("consts"), 16)
            sp.dma_start(brow[0:96, :], a["ln_b"].rearrange("l m (k p) -> (l m k) p", p=P)).then_inc(sem("consts"), 16)
            for n, name in ((96, "norm_mix_2"), (104, "norm_ffn_2"), (112, "mla_q_norm_g"), (115, "mla_kv_norm_g")):
                src = a[name].rearrange("o (k p) -> (o k) p", p=P)
                sp.dma_start(grow[n:n + src.shape[0], :], src).then_inc(sem("consts"), 16)
            sp.dma_start(fb[:, :], a["fox_b_f"].broadcast_to([P, NH])).then_inc(sem("consts"), 16)
            sp.dma_start(grow[117:121, :], a["d_skip_2"].rearrange("o (q p) -> (o q) p", p=P)).then_inc(sem("consts"), 16)
            sp.dma_start(brow[96:112, :], a["lam_re_2"][0].rearrange("(j g) p -> j (g p)", g=2)).then_inc(sem("consts"), 16)
            sp.dma_start(brow[112:128, :], a["lam_im_2"][0].rearrange("(j g) p -> j (g p)", g=2)).then_inc(sem("consts"), 16)
            sp.dma_start(ls2, a["log_step_2"][0].rearrange("(j g) -> j g", g=2)).then_inc(sem("consts"), 16)
            for n, name in enumerate(("b_re_2", "b_im_2")):
                sp.dma_start(brr[:, n], a[name][0].rearrange("(j g) p h -> (g p) j h", g=2)).then_inc(sem("consts"), 16)
            for n, name in enumerate(("c_re_2", "c_im_2")):
                sp.dma_start(cc[:, :, n, :], a[name][0].rearrange("(q g) h p -> (g h) q p", q=4)).then_inc(sem("consts"), 16)
            sp.dma_start(snk[:, 0, :], a["sinks_2"].broadcast_to([P, 8])).then_inc(sem("consts"), 16)
            for st in plan:
                kind, u = st["kind"], st["u"]
                if kind == "ff":
                    w1 = a["w_ff1_2"][0].rearrange(rows, p=P)
                    w2 = a["w_ff2_2"][0].rearrange(rows, p=P)
                    load(sp, u, u, w1[:, :, 0:256], W)
                    with sp.Fori(0, 5) as i:
                        for j in range(3):
                            v = u + 1 + 2 * j
                            load(sp, i * 6 + v, v, w1[:, :, bass.ds(i * 768 + 256 * (j + 1), 256)], W)
                            load(sp, i * 6 + v + 1, v + 1, w2[:, bass.ds(i * 6 + 2 * j, 2), :], W)
                    load(sp, u + 31, u + 31, w2[:, 30:32, :], W)
                    sp.wait_ge(sem("unit_used"), u)
                    sp.dma_start(selcum_all[:, 0:DM], a["norm_final_2"].rearrange("(o n) -> o n", o=1).broadcast_to([P, DM])).then_inc(sem("gain_in"), 16)
                    continue
                per = len(sources(st, 0))
                if not per:
                    continue
                turns = st["units"] // per
                for j, src in enumerate(sources(st, 0)):
                    if u + j >= SLOTS:
                        load(sp, u + j, u + j, src, widths[u + j])
                if turns > 1:
                    with sp.Fori(1, turns) as i:
                        for j, src in enumerate(sources(st, i)):
                            load(sp, i * per + (u + j), u + j + per, src, widths[u + j])
            sp.wait_ge(sem("out_ready"), 2)
            sp.dma_start(out[0].rearrange("(t p) n -> p t n", p=P), xn[:, :, :]).then_inc(sem("out_done"), 16)
            sp.wait_ge(sem("out_done"), 16)

        @block.gpsimd
        def _(pool):
            def rope(buf, off, half, table, A, H, n):
                pool.wait_ge(sem("rope_done"), n + 1)
                sh = [P, A, H, half]
                x1, x2 = buf[:, :, :, off:off + half], buf[:, :, :, off + half:off + 2 * half]
                c, s = (bc(table[:, m], 2, sh) for m in range(2))
                size = A * H * half
                tmp = [rt[:, m, 0:size].rearrange("p (a h d) -> p a h d", a=A, h=H) for m in range(4)]
                for o, p0, p1 in zip(tmp, (x1, x2, x1, x2), (c, s, s, c)):
                    last = pool.tensor_tensor(o, p0, p1, ALU.mult)
                last.then_inc(sem("rope_half"), 1)
                pool.wait_ge(sem("rope_half"), n + 1)
                pool.tensor_tensor(x1, tmp[0], tmp[1], ALU.subtract)
                pool.tensor_tensor(x2, tmp[2], tmp[3], ALU.add).then_inc(sem("rope_done"), 1)

            for name, n in CREDITS["gpsimd"].items():
                pool.sem_inc(sem(name), n)
            pool.memset(ones[:, :], 1.0).then_inc(sem("pool_consts"), 1)
            pool.memset(mhalf[:, :], -0.5).then_inc(sem("pool_consts"), 1)
            pool.memset(halfpi[:, :], float(np.float32(np.pi / 2))).then_inc(sem("pool_consts"), 1)
            pool.wait_ge(sem("pool_consts"), 3)
            pool.wait_ge(sem("consts"), N_CONSTS)
            for st in plan:
                kind, B = st["kind"], st["base"]
                b = B.get
                ropes = b("rope_done") - 1
                if kind in ("norm", "final"):
                    for t in range(NT):
                        pool.wait_ge(sem("var_ready"), b("var_ready", 0) + t + 1)
                        pool.tensor_tensor(rstd[:, t, 0:1], ve[:, t, 0:1], mhalf[:, 0:1], ALU.pow).then_inc(sem("rstd_ready"), 1)
                if kind in ("norm", "init") and "rms" not in st:
                    for m in range(4):
                        n = 2 * (m // 2) + 2
                        done = "xt_dve" if m % 2 == 0 else "xt_act"
                        pool.wait_ge(sem(done), b(done, 0) + n)
                        pool.tensor_scalar(cx[:, 2 * m:2 * m + 2, :], xT[:, 2 * m:2 * m + 2, :], st["c"], 1.0, ALU.mult, ALU.mult).then_inc(sem("cx_ready"), 1)
                if kind == "index":
                    n = st["j"]
                    pool.wait_ge(sem("ix_moved"), 2 * n + 2)
                    pool.wait_ge(sem("ix_kw"), n + 1)
                    rope(qk_tm[:, 0:1024].rearrange("p (a h d) -> p a h d", a=4, h=4), 0, 8, rope_p, 4, 4, ropes)
                    kid = qk_tm[:, 1024:1280].rearrange("p (t h d) -> p t h d", t=NT, h=2)
                    rope(kid[:, :, 0:1, :], 0, 8, rope_p[:, :, 0:2], NT, 1, ropes + 1)
                    pool.wait_ge(sem("rope_done"), ropes + 3)
                    pool.tensor_copy(kid[:, :, 1, :], kid[:, :, 0, :]).then_inc(sem("ix_roped"), 1)
                if kind == "ffn" and st["layer"] == 2 and st["w"] == 1:
                    pool.wait_ge(sem("prm_ready"), 1)
                    pc = Chain(pool, sem("pool_chain"))
                    A, Bk, C = (v.rearrange("p (j s) -> p j s", j=4) for v in (xn[:, 0, :], xn[:, 1, :], flat[:, 0:1024]))
                    tr = bc(ramp[:, :], 1, [P, 4, S])
                    for g in range(4):
                        phh = bc(prm[:, PHH, 4 * g:4 * g + 4], 2, [P, 4, S])
                        phl = bc(prm[:, PHL, 4 * g:4 * g + 4], 2, [P, 4, S])
                        pc.step(pool.tensor_tensor(A, tr, phh, ALU.mult))
                        pc.step(pool.tensor_scalar(Bk, A, INV2PI, ROUND, ALU.mult, ALU.add))
                        pc.step(pool.tensor_scalar(Bk, Bk, -ROUND, 1.0, ALU.add, ALU.mult))
                        for part in (PI1, PI2, PI3):
                            pc.step(pool.tensor_scalar(C, Bk, -part, 1.0, ALU.mult, ALU.mult))
                            pc.step(pool.tensor_tensor(A, A, C, ALU.add))
                        pc.step(pool.tensor_tensor(C, tr, phl, ALU.mult))
                        pc.step(pool.tensor_tensor(A, A, C, ALU.add))
                        pc.step(pool.tensor_scalar(sinT[:, 4 * g:4 * g + 4, :], A, PI_IN, -PI_IN, ALU.min, ALU.max))
                    pool.sem_inc(sem("angles"), 1)
                if kind == "ssm":
                    pc = Chain(pool, sem("ssm_pool"))
                    for n in range(16):
                        pool.wait_ge(sem("g_scan"), n + 1)
                        if n:
                            pool.wait_ge(sem("h_made"), n)
                        if n >= 2:
                            pool.wait_ge(sem("y_used"), n - 1)
                        g, h = gv[n % 2], hv[n % 2]
                        c, s = (bc(v, 1, [P, 2, S]) for v in (cosT(n), sinT[:, n, :]))
                        pool.tensor_tensor(pa, g, c, ALU.mult)
                        pc.step(pool.tensor_tensor(pb, g, s, ALU.mult))
                        pool.tensor_tensor(h[:, 0, :], pa[:, 0, :], pb[:, 1, :], ALU.subtract)
                        pool.tensor_tensor(h[:, 1, :], pa[:, 1, :], pb[:, 0, :], ALU.add).then_inc(sem("h_made"), 1)
                if kind == "latent":
                    for t in range(NT):
                        pool.wait_ge(sem("la_var"), t + 1)
                        pool.tensor_tensor(rstd[:, t, :], ve[:, t, :], mhalf[:, :], ALU.pow).then_inc(sem("la_rstd"), 1)
                    pool.wait_ge(sem("la_kr"), 1)
                    rope(kr[:, :, :].unsqueeze(2), 0, RP // 2, rope_m, NT, 1, ropes)
                    pool.wait_ge(sem("rope_done"), ropes + 2)
                    ktm = qk_tm[:, NT * 4 * MD:].rearrange("p (t h d) -> p t h d", t=NT, h=4)
                    pool.tensor_copy(ktm[:, :, :, DH:MD], bc(kr[:, :, :], 2, [P, NT, 4, RP])).then_inc(sem("la_krope"), 1)
                if kind == "attn":
                    mla = st["mix"] == "mla"
                    D = MD if mla else DH
                    moved = 3 if mla else 2

                    def turn(q, r0):
                        if st["mix"] == "fox":
                            return
                        pool.wait_ge(sem("qk_moved"), q * moved + (b("qk_moved", 0) + 2 if not mla else b("qk_moved", 0) + 1))
                        if mla:
                            v = qk_tm[:, 0:NT * 4 * MD].rearrange("p (a h d) -> p a h d", a=NT, h=4)
                            rope(v, DH, RP // 2, rope_m, NT, 4, q + r0)
                        else:
                            v = qk_tm[:, 0:4 * 4 * DH].rearrange("p (a h d) -> p a h d", a=4, h=4)
                            rope(v, 0, 8, rope_p, 4, 4, q + r0)

                    def scale(q, h):
                        pool.wait_ge(sem("rs_ready"), q * 4 + (b("rs_ready", 0) + h + 1))
                        pool.tensor_tensor(pr[:, h % 2, 0:P], pr[:, h % 2, 0:P], rs[:, h % 2, 0:1].broadcast_to([P, P]), ALU.mult)
                        pool.tensor_tensor(pr[:, h % 2, P:], pr[:, h % 2, P:], rs[:, h % 2, 1:2].broadcast_to([P, S]), ALU.mult).then_inc(sem("p_ready"), 1)

                    def quad(q, nxt):
                        scale(q, 0)
                        scale(q, 1)
                        if nxt:
                            turn(q + 1, ropes)
                        scale(q, 2)
                        scale(q, 3)

                    if "col" in st:
                        for q in range(NQ2):
                            quad(q, False)
                        continue
                    turn(0, ropes)
                    with pool.Fori(0, NG - 1) as q:
                        quad(q, True)
                    quad(NG - 1, False)

        @block.scalar
        def _(act):
            for name, n in CREDITS["scalar"].items():
                act.sem_inc(sem(name), n)
            act.wait_ge(sem("consts"), N_CONSTS)
            act.wait_ge(sem("pool_consts"), 3)
            for u in range(SLOTS):
                split_hi(act, 0, u)
            act.wait_ge(sem("gains_ready"), 2)
            act.activation(prm[:, DT, :], prm[:, LS, :], ACT.Exp).then_inc(sem("prm_act"), 1)
            act.wait_ge(sem("prm_dve"), 1)
            act.activation(prm[:, RHO, :], prm[:, AL, :], ACT.Exp).then_inc(sem("prm_act"), 1)
            act.wait_ge(sem("prm_dve"), 2)
            act.activation(prm[:, SI, :], prm[:, PHR, :], ACT.Sin)
            act.activation(prm[:, T0, :], prm[:, PHR, :], ACT.Abs).then_inc(sem("prm_act"), 1)
            act.wait_ge(sem("prm_act"), 3)
            act.activation(prm[:, CO, :], prm[:, T0, :], ACT.Sin, scale=-1.0, bias=halfpi[:, :]).then_inc(sem("prm_act"), 1)
            for st in plan:
                kind, B, u = st["kind"], st["base"], st["u"]
                b = B.get

                if st.get("keep"):
                    act.wait_ge(sem("var_ready"), b("var_ready", 0) + 2)
                    act.activation(x2[:, :, :], y[:, :, :, :].rearrange("p t n c -> p t (n c)"), ACT.Copy).then_inc(sem("kept"), 1)
                if kind in ("norm", "final"):
                    for t in range(NT):
                        act.wait_ge(sem("nmr_ready"), b("nmr_ready", 0) + t + 1)
                        act.activation(xn[:, t, 0:512], y[:, t, 0, :], ACT.Identity, bias=nmr[:, t:t + 1],
                                       scale=rstd[:, t, 0:1]).then_inc(sem("xn_act"), 1)
                if kind in ("norm", "init"):
                    if kind == "init":
                        act.wait_ge(sem("gains_ready"), 1)
                    for m in range(4):
                        k = 4 * (m // 2) + 2 + m % 2
                        act.wait_ge(sem("t_done"), b("t_done", 0) + 3 + m // 2)
                        if kind == "init":
                            act.activation(xT[:, k, :], tb[:, k, :], ACT.Copy).then_inc(sem("xt_act"), 1)
                        else:
                            g = 8 * st["g"] + k
                            act.activation(xT[:, k, :], tb[:, k, :], ACT.Identity,
                                           bias=0.0 if "rms" in st else shifts[:, g:g + 1],
                                           scale=gains[:, g:g + 1]).then_inc(sem("xt_act"), 1)
                        if m % 2:
                            for n in (m - 1, m):
                                done = "xt_dve" if n % 2 == 0 else "xt_act"
                                act.wait_ge(sem(done), b(done, 0) + m + 1)
                                act.activation(xh[:, 2 * n:2 * n + 2, :], xT[:, 2 * n:2 * n + 2, :], ACT.Copy).then_inc(sem("xh_ready"), 1)

                if kind == "ffn":
                    with act.Fori(0, FIT) as i:
                        d = (i, 3)
                        act.wait_ge(sem("unit_used"), i * 3 + (u + 1))
                        act.activation(sg[:, :, :], ps[:, 4, :].rearrange("p (c s) -> p c s", c=2), ACT.Silu).then_inc(sem("silu_done"), 1)
                        split_hi(act, d, u + 3)
                        for c in range(2):
                            act.wait_ge(sem("g_made"), i * 2 + (b("g_made", 0) + c + 1))
                            act.activation(oh[:, c, :], gt[:, c, :], ACT.Copy).then_inc(sem("gh_ready"), 1)
                        split_hi(act, d, u + 4)
                        split_hi(act, d, u + 5)

                if kind == "index":
                    n = st["j"]
                    for m in range(2):
                        act.wait_ge(sem("unit_used"), u + m + 1)
                        act.activation(qk_tm[:, 512 * m:512 * m + 512], ps[:, m, :], ACT.Copy).then_inc(sem("ix_moved"), 1)
                        split_hi(act, 0, u + m + 3)
                    split_hi(act, 0, u + 5)
                    act.wait_ge(sem("ix_t"), 3 * n + 2)
                    act.activation(qkT[:, 1, :], ps[:, 6, :], ACT.Copy).then_inc(sem("ix_q1"), 1)
                    for h in range(8):
                        act.wait_ge(sem("ix_dots"), 8 * n + h + 1)
                        if h >= 2:
                            act.wait_ge(sem("ix_acc"), 8 * n + h - 1)
                        act.activation(pr[:, h % 2, :], ps[:, 3 + h % 2, 0:3 * P], ACT.Relu, scale=0.125).then_inc(sem("ix_relu"), 1)

                if kind == "forget":
                    split_hi(act, 0, u + 3)
                    act.wait_ge(sem("fg_z"), 1)
                    act.activation(m8z[:, 0], zf[:, 0], ACT.Abs).then_inc(sem("fg_a"), 1)
                    act.wait_ge(sem("fg_a"), 1)
                    act.activation(m8z[:, 1], m8z[:, 0], ACT.Exp, scale=-1.0).then_inc(sem("fg_a"), 1)
                    act.wait_ge(sem("fg_a"), 2)
                    act.activation(m8z[:, 2], m8z[:, 1], ACT.Ln, bias=1.0).then_inc(sem("fg_l"), 1)

                if kind == "latent":
                    for m in range(3):
                        split_hi(act, 0, u + m + 3)
                    act.wait_ge(sem("la_c"), 5)
                    act.activation(xh[:, 0:5, :], xT[:, 0:5, :], ACT.Copy).then_inc(sem("la_ch"), 1)

                if kind == "attn":
                    mla = st["mix"] == "mla"
                    D = MD if mla else DH
                    moved = 3 if mla else 2
                    R = 8 if mla else 6
                    tm = qk_tm[:, 0:2 * NT * 4 * D].rearrange("p (a t h d) -> p a t h d", a=2, t=NT, h=4)
                    sc = (D ** -0.5)

                    def copy(q, j, d):
                        act.wait_ge(sem("unit_used"), q * 3 + (u + j + 1))
                        back = b("x_filled") - R + (4 if mla else 2)
                        if "col" in st:
                            back = b("x_filled")
                        act.wait_ge(sem("x_filled"), max(q * R + back, 1) if isinstance(q, int) else q * R + back)
                        if "col" in st and j == 2:
                            src = ps[:, 2, :].rearrange("p (t g d) -> p t g d", t=NT, g=4)[:, :, 0:2, :]
                            for n in range(2):
                                o = kd[:, :, :, n, :]
                                act.activation(o, src, ACT.Copy).then_inc(sem("qk_moved"), 1)
                        elif mla and j == 0:
                            o = qk_tm[:, 0:NT * 4 * MD].rearrange("p (t c) -> p t c", t=NT)
                            act.activation(o, ps[:, 0:2, 0:384], ACT.Copy).then_inc(sem("qk_moved"), 1)
                        elif mla:
                            src = ps[:, 2, :].rearrange("p (t h d) -> p t h d", t=NT, h=2)[:, :, :, 0:DH]
                            act.activation(tm[:, 1, :, 2 * j - 2:2 * j, 0:DH], src, ACT.Copy).then_inc(sem("qk_moved"), 1)
                        elif j < 2:
                            act.activation(qk_tm[:, 512 * j:512 * j + 512], ps[:, j, :], ACT.Copy).then_inc(sem("qk_moved"), 1)

                    def exps(q, h):
                        act.wait_ge(sem("nb_ready"), q * 4 + (b("nb_ready", 0) + h + 1))
                        if st["mix"] == "swa":
                            act.activation(esk[:, h % 2, :], nb[:, h % 2, :], ACT.Exp, bias=snk[:, 0, 4 * q + h:4 * q + h + 1])
                        r = (4 if mla else 2) + h - 2 if h >= 2 else (R - 2 + h) - R
                        act.wait_ge(sem("x_filled"), q * R + (b("x_filled") + r + 1))
                        act.activation(pr[:, h % 2, 0:P], s_sb[:, h % 2, 0:P], ACT.Exp, bias=nb[:, h % 2, 0:1],
                                       scale=sc, accum_out=sm[:, h % 2, 0:1])
                        act.activation(pr[:, h % 2, P:], s_sb[:, h % 2, P:], ACT.Exp, bias=nb[:, h % 2, 1:2],
                                       scale=sc, accum_out=sm[:, h % 2, 1:2]).then_inc(sem("exp_done"), 1)

                    def move(q, r, dst):
                        act.wait_ge(sem("x_filled"), q * R + (b("x_filled", 0) + r + 1))
                        act.activation(dst, ps[:, 6, :][0:dst.partition_size(), 0:dst.free_size()], ACT.Copy).then_inc(sem("x_moved1"), 1)

                    def outp(q, m):
                        act.wait_ge(sem("av_done"), q * 4 + (b("av_done", 0) + 2 * m + 2))
                        k = 2 * q + (m + st.get("out", 0))
                        act.activation(oh[:, bass.ds(k, 1), :], ps[:, 7, 0:S].unsqueeze(1), ACT.Copy).then_inc(sem("oh_ready"), 1)

                    def quad(q, nxt):
                        d = (q, 3) if nxt else None
                        if mla:
                            move(q, 1, qkT[0:MD, 1, :])
                        if nxt:
                            copy(q + 1, 0, d)
                            split_hi(act, d, u + 6)
                        exps(q, 0)
                        exps(q, 1)
                        move(q, 3 if mla else 1, qkT[0:MD, 3, :] if mla else qkT[:, 1, :])
                        if nxt:
                            copy(q + 1, 1, d)
                            split_hi(act, d, u + 7)
                        pt0 = 4 if mla else 2
                        move(q, pt0 + 1, pT[:, 1, :])
                        exps(q, 2)
                        exps(q, 3)
                        outp(q, 0)
                        if nxt:
                            if mla:
                                copy(q + 1, 2, d)
                            split_hi(act, d, u + 8)
                        move(q, pt0 + 3, pT[:, 1, :])
                        outp(q, 1)

                    for j in range(3):
                        if j < 2 or mla:
                            copy(0, j, 0)
                        split_hi(act, 0, u + j + 3)
                    if "col" in st:
                        copy(0, 2, 0)
                        for q in range(NQ2):
                            quad(q, False)
                        continue
                    with act.Fori(0, NG - 1) as q:
                        quad(q, True)
                    quad(NG - 1, False)

                if kind in ("oproj", "oproj2"):
                    for m in range(4):
                        split_hi(act, 0, u + m + 3)

                if kind == "ssm_in":
                    for m in range(2):
                        act.wait_ge(sem("unit_used"), u + m + 1)
                        act.activation(qk_tm[:, 512 * m:512 * m + 512], ps[:, m, :], ACT.Copy).then_inc(sem("u_moved"), 1)
                        split_hi(act, 0, u + m + 3)
                    act.wait_ge(sem("angles"), 1)
                    for m, o in enumerate((xn[:, :, :].rearrange("p t c -> p (t c)"), xT[:, :, :].rearrange("p k s -> p (k s)"))):
                        src = selcum_all[:, 2048 * m:2048 * m + 2048]
                        act.activation(o, src, ACT.Abs).then_inc(sem("trig"), 1)
                        act.wait_ge(sem("trig"), 2 * m + 1)
                        act.activation(o, o, ACT.Sin, scale=-1.0, bias=halfpi[:, :]).then_inc(sem("trig"), 1)
                    act.activation(selcum_all[:, :], selcum_all[:, :], ACT.Sin).then_inc(sem("trig"), 1)

                if kind == "ssm":
                    def blocks(q):
                        act.wait_ge(sem("bt_turned"), q + 1)
                        if q:
                            act.wait_ge(sem("x_made"), 4 * q)
                        for m in range(2):
                            ins = act.activation(BT[:, 4 * m:4 * m + 4, :].rearrange("p a c -> p (a c)"), ps[:, m, :], ACT.Copy)
                        ins.then_inc(sem("bt_moved"), 1)

                    def gelu(q):
                        act.wait_ge(sem("ys_made"), q + 1)
                        if q:
                            act.wait_ge(sem("gel_lo"), q)
                        act.activation(acc[:, 0:S], ysT[:, q % 2, :], ACT.Gelu_apprx_tanh).then_inc(sem("gelu_done"), 1)
                        act.wait_ge(sem("gelu_done"), q + 1)
                        act.activation(bh[:, q, :], acc[:, 0:S], ACT.Copy).then_inc(sem("gel_hi"), 1)

                    blocks(0)
                    for q in range(1, 4):
                        blocks(q)
                        gelu(q - 1)
                    gelu(3)

                if kind == "glu":
                    for m in range(2):
                        split_hi(act, 0, u + m + 3)
                    for m in range(2):
                        act.wait_ge(sem("glu_done"), 1)
                        act.activation((sg, gt)[m][:, :, :].rearrange("p a s -> p (a s)"), ps[:, 2 + m, :], ACT.Sigmoid).then_inc(sem("glu_sig"), 1)
                    for m in range(2):
                        act.wait_ge(sem("glu_made"), m + 1)
                        act.activation(bh[:, 2 * m:2 * m + 2, :], qkT[:, m, :].rearrange("p (k s) -> p k s", k=2), ACT.Copy).then_inc(sem("glu_hi"), 1)

                if kind == "branches":
                    for J in range(2):
                        for m in range(3):
                            split_hi(act, 0, u + 9 * J + m + 3)
                        for g in range(6 * J, 6 * J + 6):
                            act.wait_ge(sem("unit_used"), u + 3 * J + g + 4)
                            if g >= 2:
                                act.wait_ge(sem("gate_used"), g - 1)
                            act.activation((sg, gt)[g % 2][:, :, :].rearrange("p a s -> p (a s)"), ps[:, 6 + g % 2, :], ACT.Sigmoid).then_inc(sem("gate_sig"), 1)
                            split_hi(act, 0, u + 3 * J + g + 6)
                    for m in range(4):
                        act.wait_ge(sem("mixed"), m + 1)
                        if m == 0:
                            act.wait_ge(sem("unit_used"), u + 18)
                        act.activation(xh[:, 2 * m:2 * m + 2, :], xT[:, 2 * m:2 * m + 2, :], ACT.Copy).then_inc(sem("mix_hi"), 1)

                if kind == "ff":
                    def relu(i, j, k0):
                        act.wait_ge(sem("unit_used"), i * 6 + (u + (2 * k0 if k0 else 1)))
                        act.activation(flat[:, 512 * j:512 * j + 512], ps[:, 4 + j, :], ACT.Relu).then_inc(sem("relu_done"), 1)

                    def high(i, j, k0):
                        act.wait_ge(sem("sq_done"), i * 3 + (k0 + 1))
                        if k0 >= 3:
                            act.wait_ge(sem("unit_used"), i * 6 + (u + 2 * (k0 - 3) + 3))
                        act.activation(oh[:, 2 * j:2 * j + 2, :], xT[:, 2 * j:2 * j + 2, :], ACT.Copy).then_inc(sem("fh_ready"), 1)

                    def turn(i, j, k0, d, splits):
                        relu(i, (j + 1) % 3, k0 + 1)
                        if splits:
                            split_hi(act, d, u + 1 + 2 * k0 + 3)
                        high(i, (j + 1) % 3, k0 + 1)
                        if splits:
                            split_hi(act, d, u + 2 + 2 * k0 + 3)

                    relu(0, 0, 0)
                    split_hi(act, 0, u + 3)
                    high(0, 0, 0)
                    for k0 in range(3):
                        turn(0, k0, k0, 0, True)
                    with act.Fori(0, 3) as i:
                        for j in range(3):
                            turn(i, j, 3 + j, (i, 6), True)
                    for k0 in (12, 13, 14):
                        turn(0, k0 % 3, k0, 0, k0 < 14)

        @block.vector
        def _(dve):
            for name, n in CREDITS["vector"].items():
                dve.sem_inc(sem(name), n)
            dve.wait_ge(sem("consts"), N_CONSTS)
            ch = Chain(dve, sem("dve_chain"))
            dve.tensor_copy(ls16[:, :, :], bc(ls2, 2, [16, 2, 64])).then_inc(sem("steps_spread"), 1)
            dve.wait_ge(sem("g_t"), 1)
            dve.tensor_copy(gains[:, 0:121], ps[:, 4, 0:121])
            dve.tensor_copy(shifts[:, :], ps[:, 4, 128:256])
            dve.tensor_copy(prm[:, LR, :], ps[:, 4, 224:240])
            dve.tensor_copy(prm[:, LI, :], ps[:, 4, 240:256]).then_inc(sem("gains_ready"), 1)
            dve.tensor_copy(prm[:, LS, :], ps[:, 5, 0:16]).then_inc(sem("gains_ready"), 1)
            dve.wait_ge(sem("gains_ready"), 2)
            for u in range(SLOTS):
                split_lo(dve, 0, u)
            R_ = lambda n: prm[:, n, :]
            tt, ts, stt = dve.tensor_tensor, dve.tensor_scalar, dve.scalar_tensor_tensor
            ch.step(ts(snk[:, 1, :], snk[:, 0, :], 8.0, None, ALU.mult))
            dve.wait_ge(sem("prm_act"), 1)
            tt(R_(PH), R_(LI), R_(DT), ALU.mult)
            tt(R_(AL), R_(LR), R_(DT), ALU.mult).then_inc(sem("prm_dve"), 1)
            dve.wait_ge(sem("prm_dve"), 1)
            ch.step(ts(R_(T1), R_(PH), INV2PI, ROUND, ALU.mult, ALU.add))
            ch.step(ts(R_(T1), R_(T1), -ROUND, None, ALU.add))
            ch.step(stt(R_(PHR), R_(T1), -PI1, R_(PH), ALU.mult, ALU.add))
            ch.step(stt(R_(PHR), R_(T1), -PI2, R_(PHR), ALU.mult, ALU.add))
            ch.step(stt(R_(PHR), R_(T1), -PI3, R_(PHR), ALU.mult, ALU.add))
            ts(R_(PHR), R_(PHR), PI_IN, -PI_IN, ALU.min, ALU.max).then_inc(sem("prm_dve"), 1)
            dve.wait_ge(sem("prm_dve"), 2)
            ch.step(ts(R_(PHH), R_(PHR), 1536.0, None, ALU.add))
            ch.step(ts(R_(PHH), R_(PHH), -1536.0, None, ALU.add))
            tt(R_(PHL), R_(PHR), R_(PHH), ALU.subtract).then_inc(sem("prm_ready"), 1)
            dve.wait_ge(sem("prm_act"), 4)
            ch.step(tt(R_(NR), R_(RHO), R_(CO), ALU.mult))
            ch.step(ts(R_(NR), R_(NR), -1.0, None, ALU.add))
            ch.step(tt(R_(NI), R_(RHO), R_(SI), ALU.mult))
            ch.step(tt(R_(T1), R_(LR), R_(LR), ALU.mult))
            ch.step(tt(R_(T2), R_(LI), R_(LI), ALU.mult))
            ch.step(tt(R_(T1), R_(T1), R_(T2), ALU.add))
            ch.step(dve.reciprocal(R_(DEN), R_(T1)))
            for out_, x1, x2_, op in ((FR, (NR, LR), (NI, LI), ALU.add), (FI, (NI, LR), (NR, LI), ALU.subtract)):
                ch.step(tt(R_(T1), R_(x1[0]), R_(x1[1]), ALU.mult))
                ch.step(tt(R_(T2), R_(x2_[0]), R_(x2_[1]), ALU.mult))
                ch.step(tt(R_(T1), R_(T1), R_(T2), op))
                ch.step(tt(R_(out_), R_(T1), R_(DEN), ALU.mult))
            fr, fi = (bc(R_(n), 2, [P, 16, 16]) for n in (FR, FI))
            tmp = pT[:, 0, 0:256].rearrange("p (j h) -> p j h", j=16)
            for n, (g1, g2, op) in enumerate(((fr, fi, ALU.subtract), (fi, fr, ALU.add))):
                ch.step(tt(tmp, brr[:, 1], g2, ALU.mult))
                ch.step(tt(bb[:, n], brr[:, 0], g1, ALU.mult))
                ch.step(tt(bb[:, n], bb[:, n], tmp, op))
            for st in plan:
                kind, B, u = st["kind"], st["base"], st["u"]
                b = B.get

                if kind in ("norm", "final"):
                    dve.wait_ge(sem("unit_used"), u)
                    if st.get("g") == 12:
                        dve.wait_ge(sem("lift_done"), 1)
                    for t in range(NT):
                        for n in range(2):
                            ch.link(dve.bn_stats(st6[:, t, n, :], y[:, t, n, :]))
                        ch.wait()
                        ch.link(dve.bn_aggr(mv[:, t, :], st6[:, t, :, :].rearrange("p a b -> p (a b)")))
                        ch.wait()
                        if "rms" in st:
                            ch.step(dve.scalar_tensor_tensor(out=mv[:, t, 1:2], in0=mv[:, t, 0:1], scalar=mv[:, t, 0:1],
                                                             in1=mv[:, t, 1:2], op0=ALU.mult, op1=ALU.add))
                        dve.tensor_scalar(ve[:, t, 0:1], mv[:, t, 1:2], st["eps"], None, ALU.add).then_inc(sem("var_ready"), 1)
                    for t in range(NT):
                        dve.wait_ge(sem("rstd_ready"), b("rstd_ready", 0) + t + 1)
                        if st.get("keep"):
                            dve.wait_ge(sem("kept"), 1)
                        dve.scalar_tensor_tensor(out=nmr[:, t:t + 1], in0=mv[:, t, 0:1], scalar=0.0 if "rms" in st else -1.0,
                                                 in1=rstd[:, t, 0:1], op0=ALU.mult, op1=ALU.mult).then_inc(sem("nmr_ready"), 1)
                        dve.wait_ge(sem("nmr_ready"), b("nmr_ready", 0) + t + 1)
                        dve.tensor_scalar(xn[:, t, 512:], y[:, t, 1, :], rstd[:, t, 0:1], nmr[:, t:t + 1],
                                          ALU.mult, ALU.add).then_inc(sem("xn_dve"), 1)
                if kind in ("norm", "init"):
                    def low(m):
                        dve.wait_ge(sem("xh_ready"), b("xh_ready", 0) + m + 1)
                        dve.tensor_tensor(xl[:, 2 * m:2 * m + 2, :], xT[:, 2 * m:2 * m + 2, :],
                                          xh[:, 2 * m:2 * m + 2, :].bitcast(F32), ALU.subtract).then_inc(sem("xl_ready"), 1)

                    for m in range(4):
                        k = 4 * (m // 2) + m % 2
                        dve.wait_ge(sem("t_done"), b("t_done", 0) + 3 + m // 2)
                        if m == 0:
                            if b("cx_ready", 0):
                                dve.wait_ge(sem("cx_ready"), b("cx_ready", 0))
                        if kind == "init":
                            dve.tensor_copy(xT[:, k, :], tb[:, k, :]).then_inc(sem("xt_dve"), 1)
                        else:
                            g = 8 * st["g"] + k
                            dve.tensor_scalar(xT[:, k, :], tb[:, k, :], gains[:, g:g + 1],
                                              0.0 if "rms" in st else shifts[:, g:g + 1],
                                              ALU.mult, ALU.add).then_inc(sem("xt_dve"), 1)
                        if m == 3:
                            low(0)
                            low(1)
                    low(2)
                    low(3)

                if kind == "ffn":
                    with dve.Fori(0, FIT) as i:
                        d = (i, 3)
                        for c in range(2):
                            if c == 0:
                                dve.wait_ge(sem("silu_done"), i + (b("silu_done", 0) + 1))
                                dve.wait_ge(sem("up0_done"), i + (b("up0_done", 0) + 1))
                            else:
                                dve.wait_ge(sem("unit_used"), i * 3 + (u + 2))
                            dve.tensor_tensor(gt[:, c, :], sg[:, c, :], ps[:, 5 + c, 0:S], ALU.mult).then_inc(sem("g_made"), 1)
                            dve.wait_ge(sem("gh_ready"), i * 2 + (b("gh_ready", 0) + c + 1))
                            dve.tensor_tensor(ol[:, c, :], gt[:, c, :], oh[:, c, :].bitcast(F32), ALU.subtract).then_inc(sem("gl_ready"), 1)
                            split_lo(dve, d, u + 3 + c)
                        split_lo(dve, d, u + 5)

                if kind == "index":
                    n = st["j"]
                    for m in range(2):
                        split_lo(dve, 0, u + m + 3)
                    dve.wait_ge(sem("unit_used"), u + 3)
                    kw = ps[:, 2, 0:144].rearrange("p (t c) -> p t c", t=NT)
                    kid = qk_tm[:, 1024:1280].rearrange("p (t h d) -> p t h d", t=NT, h=2)
                    dve.tensor_copy(kid[:, :, 0, :], kw[:, :, 0:64])
                    dve.tensor_scalar(wi[:, :, :], kw[:, :, 64:72], float(np.float32(8 ** -0.5)), None, ALU.mult).then_inc(sem("ix_kw"), 1)
                    split_lo(dve, 0, u + 5)
                    ch.link(dve.memset(acc[:, :], 0.0))
                    dve.wait_ge(sem("ix_t"), 3 * n + 1)
                    dve.tensor_copy(qkT[:, 0, :], ps[:, 5, :])
                    dve.wait_ge(sem("ix_t"), 3 * n + 3)
                    dve.tensor_copy(qkT[:, 2, 0:S], ps[:, 7, 0:S]).then_inc(sem("ix_k"), 1)
                    ch.wait()
                    for h in range(8):
                        dve.wait_ge(sem("ix_relu"), 8 * n + h + 1)
                        if h:
                            dve.wait_ge(sem("ix_acc"), 8 * n + h)
                        for t, c0, c1 in ((0, 0, P), (1, P, 3 * P)):
                            last = dve.scalar_tensor_tensor(out=acc[:, c0:c1], in0=pr[:, h % 2, c0:c1],
                                                            scalar=wi[:, t, h:h + 1], in1=acc[:, c0:c1],
                                                            op0=ALU.mult, op1=ALU.add)
                        last.then_inc(sem("ix_acc"), 1)
                    dve.wait_ge(sem("ix_acc"), 8 * n + 8)
                    ch.link(dve.tensor_tensor(acc[:, :], acc[:, :], causal[:, :], ALU.add))
                    ch.wait()
                    for r in range(TOPK // 8):
                        for t, c0, c1 in ((0, 0, P), (1, P, 3 * P)):
                            ch.link(dve.max(m8[:, t, :], acc[:, c0:c1]))
                        ch.wait()
                        for t, c0, c1 in ((0, 0, P), (1, P, 3 * P)):
                            ch.link(dve.match_replace(acc[:, c0:c1], m8[:, t, :], acc[:, c0:c1], TAKEN))
                        ch.wait()
                    ch.link(dve.tensor_scalar(bias[:, :], acc[:, :], TAKEN, NEG, ALU.not_equal, ALU.mult))
                    ch.wait()
                    ch.link(dve.tensor_tensor(bias[:, :], bias[:, :], causal[:, :], ALU.add))
                    ch.wait()

                if kind == "forget":
                    dve.wait_ge(sem("unit_used"), u + 1)
                    z = ps[:, 0, 0:32].rearrange("p (t c) -> p t c", t=NT)
                    dve.tensor_tensor(zf[:, 0], z, bc(fb[:, :], 1, [P, NT, NH]), ALU.add).then_inc(sem("fg_z"), 1)
                    dve.wait_ge(sem("fg_z"), 1)
                    ch.link(dve.tensor_scalar(zf[:, 1], zf[:, 0], 0.0, None, ALU.min))
                    split_lo(dve, 0, u + 3)
                    ch.wait()
                    dve.wait_ge(sem("fg_l"), 1)
                    dve.tensor_tensor(zf[:, 2], zf[:, 1], m8z[:, 2], ALU.subtract).then_inc(sem("fg_lf"), 1)
                    dve.wait_ge(sem("fg_cum"), 1)
                    dve.tensor_tensor(selcum[:, :, :], bc(ps[0:16, 7, 0:S], 1, [16, NH, S]),
                                      bc(ident[0:16, 0:16], 2, [16, NH, S]), ALU.mult).then_inc(sem("fg_sel"), 1)

                if kind == "latent":
                    for m in range(3):
                        split_lo(dve, 0, u + m + 3)
                    dve.wait_ge(sem("unit_used"), u + 3)
                    dve.tensor_copy(kr[:, :, :], ps[:, 2:4, 256:288]).then_inc(sem("la_kr"), 1)
                    for t in range(NT):
                        for n, part in enumerate((ps[:, t, 0:QL], ps[:, 2 + t, 0:KVL])):
                            ch.link(dve.bn_stats(st6[:, t, n, :], part))
                        ch.wait()
                        for n in range(2):
                            ch.link(dve.bn_aggr(mv[:, n, :], st6[:, t, n, :]))
                        ch.wait()
                        ch.link(dve.tensor_tensor(ve[:, t, :], mv[:, :, 0], mv[:, :, 0], ALU.mult))
                        ch.wait()
                        ch.link(dve.tensor_tensor(ve[:, t, :], ve[:, t, :], mv[:, :, 1], ALU.add))
                        ch.wait()
                        dve.tensor_scalar(ve[:, t, :], ve[:, t, :], RMS_EPS, None, ALU.add).then_inc(sem("la_var"), 1)
                    for t in range(NT):
                        dve.wait_ge(sem("la_rstd"), t + 1)
                        dve.tensor_scalar(xn[:, t, 0:QL], ps[:, t, 0:QL], rstd[:, t, 0:1], None, ALU.mult)
                        dve.tensor_scalar(xn[:, t, QL:QL + KVL], ps[:, 2 + t, 0:KVL], rstd[:, t, 1:2], None, ALU.mult).then_inc(sem("la_cn"), 1)
                    dve.wait_ge(sem("la_t"), 1)
                    for k in range(5):
                        dve.tensor_scalar(xT[:, k, :], ps[:, 5 + k // 2, (k % 2) * S:(k % 2 + 1) * S],
                                          gains[:, 112 + k:113 + k], None, ALU.mult).then_inc(sem("la_c"), 1)
                    dve.wait_ge(sem("la_ch"), 1)
                    dve.tensor_tensor(xl[:, 0:5, :], xT[:, 0:5, :], xh[:, 0:5, :].bitcast(F32), ALU.subtract).then_inc(sem("la_cl"), 1)

                if kind == "attn":
                    mla = st["mix"] == "mla"
                    R = 8 if mla else 6
                    D = MD if mla else DH
                    alibi = "col" in st

                    def mask_of(q, h):
                        if not alibi:
                            return bias if st["mix"] == "dsa" else causal
                        slope = 2.0 ** (-8.0 * (4 * q + h + 1 + (8 if st["mix"] == "moba" else 0)) / 16)
                        m = (bias, acc)[h % 2]
                        ch.step(dve.scalar_tensor_tensor(out=m[:, :], in0=distp[:, :], scalar=-8.0 * float(np.float32(slope)),
                                                         in1=(windowp if st["mix"] == "swa" else causal)[:, :],
                                                         op0=ALU.mult, op1=ALU.add))
                        return m

                    def move(q, r, dst):
                        dve.wait_ge(sem("x_filled"), q * R + (b("x_filled", 0) + r + 1))
                        dve.tensor_copy(dst, ps[:, 5, :][0:dst.partition_size(), 0:dst.free_size()]).then_inc(sem("x_moved0"), 1)

                    def front(q, h):
                        dve.wait_ge(sem("s_filled"), q * 4 + (b("s_filled", 0) + h + 1))
                        if b("exp_done", 0) or h >= 2:
                            dve.wait_ge(sem("exp_done"), q * 4 + (b("exp_done", 0) + h - 1))
                        dve.memset(tick[:, :], 0.0)
                        mask = mask_of(q, h)
                        for m, c0, c1 in ((0, 0, P), (1, P, 3 * P)):
                            last = dve.tensor_tensor_reduce(s_sb[:, h % 2, c0:c1], ps[:, 3 + h % 2, c0:c1], mask[:, c0:c1],
                                                            1.0, -3.0e38, ALU.add, ALU.max, mx[:, h % 2, m:m + 1])
                        last.then_inc(sem("masked"), 1)
                        dve.wait_ge(sem("masked"), q * 4 + (b("masked", 0) + h + 1))
                        if st["mix"] == "swa":
                            dve.tensor_scalar(nb[:, h % 2, :], mx[:, h % 2, :], snk[:, 1, 4 * q + h:4 * q + h + 1], -(D ** -0.5),
                                              ALU.max, ALU.mult).then_inc(sem("nb_ready"), 1)
                        else:
                            dve.tensor_scalar(nb[:, h % 2, :], mx[:, h % 2, :], -(D ** -0.5), None, ALU.mult).then_inc(sem("nb_ready"), 1)

                    def recip(q, h):
                        dve.wait_ge(sem("exp_done"), q * 4 + (b("exp_done", 0) + h + 1))
                        if b("p_ready", 0) or h >= 2:
                            dve.wait_ge(sem("p_ready"), q * 4 + (b("p_ready", 0) + h - 1))
                        if st["mix"] == "swa":
                            ch.step(dve.tensor_tensor(sm[:, h % 2, :], sm[:, h % 2, :], esk[:, h % 2, :], ALU.add))
                        dve.reciprocal(rs[:, h % 2, :], sm[:, h % 2, :]).then_inc(sem("rs_ready"), 1)

                    def low(q, m):
                        dve.wait_ge(sem("oh_ready"), q * 2 + (b("oh_ready", 0) + m + 1))
                        k = 2 * q + (m + st.get("out", 0))
                        dve.tensor_tensor(ol[:, bass.ds(k, 1), :], ps[:, 7, 0:S].unsqueeze(1),
                                          oh[:, bass.ds(k, 1), :].bitcast(F32), ALU.subtract).then_inc(sem("ol_ready"), 1)

                    def kv(q, j):
                        if mla:
                            dve.wait_ge(sem("unit_used"), q * 3 + (u + j + 1))
                            if j == 1 and not (isinstance(q, int) and q == 0):
                                dve.wait_ge(sem("mla_v"), q)
                            dve.wait_ge(sem("qk_moved"), q * 3 + (b("qk_moved", 0) + j + 1))
                            src = ps[:, 2, :].rearrange("p (t h d) -> p t h d", t=NT, h=2)[:, :, :, DH:]
                            dve.tensor_copy(v_nx[:, :, 2 * j - 2:2 * j, :], src).then_inc(sem("kv_moved"), 1)

                    def values(q, first):
                        if mla:
                            dve.wait_ge(sem("kv_moved"), q * 2 + 2)
                        else:
                            dve.wait_ge(sem("unit_used"), q * 3 + (u + 3))
                        if not first or b("av_done", 0):
                            dve.wait_ge(sem("av_done"), q * 4 + b("av_done", 0))
                        src = v_nx[:, :, :, :] if mla else ps[:, 2, :].rearrange("p (t h d) -> p t h d", t=NT, h=4)
                        dve.tensor_copy(v_tm[:, :, :, :], src).then_inc(sem("mla_v" if mla else "v_moved"), 1)

                    def quad(q, nxt):
                        d = (q, 3)
                        pt0 = 4 if mla else 2
                        move(q, 0, qkT[0:MD, 0, :] if mla else qkT[:, 0, :])
                        front(q, 0)
                        front(q, 1)
                        if mla:
                            move(q, 2, qkT[0:MD, 2, :])
                        if nxt:
                            split_lo(dve, d, u + 6)
                        recip(q, 0)
                        recip(q, 1)
                        move(q, pt0, pT[:, 0, :])
                        front(q, 2)
                        front(q, 3)
                        if nxt:
                            kv(q + 1, 1)
                            split_lo(dve, d, u + 7)
                        low(q, 0)
                        recip(q, 2)
                        recip(q, 3)
                        if nxt:
                            kv(q + 1, 2)
                        move(q, pt0 + 2, pT[:, 0, :])
                        if nxt:
                            split_lo(dve, d, u + 8)
                        low(q, 1)
                        if nxt:
                            values(q + 1, False)

                    for j in range(3):
                        split_lo(dve, 0, u + j + 3)
                        if mla and j:
                            kv(0, j)
                    if alibi:
                        dve.wait_ge(sem("qk_moved"), b("qk_moved", 0) + 4)
                        dve.wait_ge(sem("av_done"), b("av_done"))
                        src = ps[:, 2, :].rearrange("p (t g d) -> p t g d", t=NT, g=4)[:, :, 2:4, :]
                        dve.tensor_copy(v_tm[:, :, 0:2, :], src).then_inc(sem("v_moved"), 1)
                        for q in range(NQ2):
                            quad(q, False)
                        continue
                    values(0, True)
                    with dve.Fori(0, NG - 1) as q:
                        quad(q, True)
                    quad(NG - 1, False)

                if kind in ("oproj", "oproj2"):
                    for m in range(4):
                        split_lo(dve, 0, u + m + 3)

                if kind in ("ssm_in", "glu"):
                    for m in range(2):
                        split_lo(dve, 0, u + m + 3)

                if kind == "ssm":
                    ch.step(dve.memset(flat[:, :], 0.0))

                    def shifted(buf, r, half):
                        v = buf[half * 64:half * 64 + 64, :, r, :]
                        return [v[:, j, 32 * j + 16 * half:32 * j + 16 * half + 16] for j in range(4)]

                    def build_z(q):
                        if q:
                            dve.wait_ge(sem("bt_turned"), q)
                        for r in range(2):
                            for half in range(2):
                                for j, o in enumerate(shifted(Z, r, half)):
                                    last = dve.tensor_copy(o, bb[half * 64:half * 64 + 64, r, 4 * q + j, :])
                        last.then_inc(sem("z_built"), 1)

                    def build_cl(q):
                        dve.wait_ge(sem("bt_turned"), q + 1)
                        if q:
                            dve.wait_ge(sem("y_used"), 4 * q)
                        for r in range(2):
                            for half in range(2):
                                for j, o in enumerate(shifted(CL, r, half)):
                                    c0 = r * P + 32 * j + 16 * half
                                    last = dve.tensor_scalar(o, ps[0:64, 2, c0:c0 + 16], -1.0 if r else 1.0, None, ALU.mult)
                        last.then_inc(sem("cl_built"), 1)

                    def ys(q):
                        dve.wait_ge(sem("y_used"), 4 * q + 4)
                        if q >= 2:
                            dve.wait_ge(sem("gelu_done"), q - 1)
                        dve.scalar_tensor_tensor(out=ysT[:, q % 2, :], in0=uT[:, q, :], scalar=gains[:, 117 + q:118 + q],
                                                 in1=ps[:, 5 + q % 2, 0:S], op0=ALU.mult, op1=ALU.add).then_inc(sem("ys_made"), 1)

                    def glow(q):
                        dve.wait_ge(sem("gel_hi"), q + 1)
                        dve.tensor_tensor(bl[:, q, :], acc[:, 0:S], bh[:, q, :].bitcast(F32), ALU.subtract).then_inc(sem("gel_lo"), 1)

                    dve.wait_ge(sem("u_moved"), 2)
                    build_z(0)
                    build_cl(0)
                    dve.wait_ge(sem("trig"), 5)
                    for n in range(16):
                        q = n // 4
                        X = ps[:, 3 + n % 2, :].rearrange("p (r s) -> p r s", r=2)
                        c, s_ = (bc(v, 1, [P, 2, S]) for v in (cosT(n), sinT[:, n, :]))
                        dve.wait_ge(sem("x_made"), n + 1)
                        dve.tensor_tensor(ta[:, :, :], X, c, ALU.mult)
                        ch.step(dve.tensor_tensor(tb2[:, :, :], X, s_, ALU.mult))
                        dve.tensor_tensor(wv[:, 0, :], ta[:, 0, :], tb2[:, 1, :], ALU.add)
                        dve.tensor_tensor(wv[:, 1, :], ta[:, 1, :], tb2[:, 0, :], ALU.subtract).then_inc(sem("w_made"), 1)
                        dve.wait_ge(sem("w_made"), n + 1)
                        if n >= 2:
                            dve.wait_ge(sem("h_made"), n - 1)
                        rho = prm[:, RHO, n:n + 1].broadcast_to([P, S])
                        dve.tensor_tensor_scan(gv[n % 2][:, 0, :], rho, wv[:, 0, :], 0.0, ALU.mult, ALU.add)
                        dve.tensor_tensor_scan(gv[n % 2][:, 1, :], rho, wv[:, 1, :], 0.0, ALU.mult, ALU.add).then_inc(sem("g_scan"), 1)
                        dve.wait_ge(sem("g_scan"), n + 1)
                        if n % 4 == 1 and q < 3:
                            build_z(q + 1)
                        if n % 4 == 0 and q:
                            build_cl(q)
                            ys(q - 1)
                        if n % 4 == 2 and q:
                            glow(q - 1)
                    ys(3)
                    glow(3)

                if kind == "glu":
                    for m in range(2):
                        dve.wait_ge(sem("glu_sig"), m + 1)
                        sv = (sg, gt)[m][:, :, :].rearrange("p a s -> p (a s)")
                        dve.tensor_tensor(qkT[:, m, :], sv, ps[:, m, :], ALU.mult).then_inc(sem("glu_made"), 1)
                    for m in range(2):
                        dve.wait_ge(sem("glu_hi"), m + 1)
                        dve.tensor_tensor(bl[:, 2 * m:2 * m + 2, :], qkT[:, m, :].rearrange("p (k s) -> p k s", k=2),
                                          bh[:, 2 * m:2 * m + 2, :].bitcast(F32), ALU.subtract).then_inc(sem("glu_lo"), 1)

                if kind == "branches":
                    tmp = rt[:, :, :].rearrange("p a c -> p (a c)")
                    for J in range(2):
                        for m in range(3):
                            split_lo(dve, 0, u + 9 * J + m + 3)
                        for g in range(6 * J, 6 * J + 6):
                            jj, m = (g % 6) // 3, g % 3
                            mix = xT[:, 4 * J + 2 * jj:4 * J + 2 * jj + 2, :].rearrange("p k s -> p (k s)")
                            sv = (sg, gt)[g % 2][:, :, :].rearrange("p a s -> p (a s)")
                            dve.wait_ge(sem("gate_sig"), g + 1)
                            if m and g:
                                ch.wait()
                            dve.tensor_tensor(mix if m == 0 else tmp, sv, ps[:, 2 * m + jj, :], ALU.mult).then_inc(sem("gate_used"), 1)
                            dve.wait_ge(sem("gate_used"), g + 1)
                            if m:
                                ins = dve.tensor_tensor(mix, mix, tmp, ALU.add)
                                if m == 2:
                                    ins.then_inc(sem("mixed"), 1)
                                    dve.wait_ge(sem("mixed"), g // 3 + 1)
                                else:
                                    ch.link(ins)
                            split_lo(dve, 0, u + 3 * J + g + 6)
                    for m in range(4):
                        dve.wait_ge(sem("mix_hi"), m + 1)
                        dve.tensor_tensor(xl[:, 2 * m:2 * m + 2, :], xT[:, 2 * m:2 * m + 2, :],
                                          xh[:, 2 * m:2 * m + 2, :].bitcast(F32), ALU.subtract).then_inc(sem("mix_lo"), 1)

                if kind == "ff":
                    def square(i, j, k0):
                        dve.wait_ge(sem("relu_done"), i * 3 + (k0 + 1))
                        r = flat[:, 512 * j:512 * j + 512].rearrange("p (k s) -> p k s", k=2)
                        dve.tensor_tensor(xT[:, 2 * j:2 * j + 2, :], r, r, ALU.mult).then_inc(sem("sq_done"), 1)

                    def low(i, j, k0):
                        dve.wait_ge(sem("fh_ready"), i * 3 + (k0 + 1))
                        dve.tensor_tensor(ol[:, 2 * j:2 * j + 2, :], xT[:, 2 * j:2 * j + 2, :],
                                          oh[:, 2 * j:2 * j + 2, :].bitcast(F32), ALU.subtract).then_inc(sem("fl_ready"), 1)

                    def turn(i, j, k0, d, splits):
                        square(i, (j + 1) % 3, k0 + 1)
                        if splits:
                            split_lo(dve, d, u + 1 + 2 * k0 + 3)
                        low(i, (j + 1) % 3, k0 + 1)
                        if splits:
                            split_lo(dve, d, u + 2 + 2 * k0 + 3)

                    square(0, 0, 0)
                    split_lo(dve, 0, u + 3)
                    low(0, 0, 0)
                    for k0 in range(3):
                        turn(0, k0, k0, 0, True)
                    with dve.Fori(0, 3) as i:
                        for j in range(3):
                            turn(i, j, 3 + j, (i, 6), True)
                    for k0 in (12, 13, 14):
                        turn(0, k0 % 3, k0, 0, k0 < 14)

                if kind == "final":
                    dve.wait_ge(sem("gain_in"), 16)
                    for t in range(NT):
                        dve.wait_ge(sem("xn_act"), b("xn_act") + t + 1)
                        dve.wait_ge(sem("xn_dve"), b("xn_dve") + t + 1)
                        dve.tensor_tensor(xn[:, t, :], xn[:, t, :], selcum_all[:, 0:DM], ALU.mult).then_inc(sem("out_ready"), 1)

        @block.tensor
        def _(pe):
            def used(ins):
                ins.then_inc(sem("unit_used"), 1)

            for name, n in CREDITS["tensor"].items():
                pe.sem_inc(sem(name), n)
            pe.wait_ge(sem("consts"), N_CONSTS)
            pe.wait_ge(sem("pool_consts"), 3)
            pe.wait_ge(sem("steps_spread"), 1)
            pe.transpose(ps[:, 4, 0:121], grow[0:121, :], ident[0:121, 0:121])
            pe.transpose(ps[:, 5, 0:16], ls16[:, :, :].rearrange("p g d -> p (g d)"), ident[0:16, 0:16])
            pe.transpose(ps[:, 4, 128:256], brow[:, :], ident[:, :]).then_inc(sem("g_t"), 1)
            for st in plan:
                kind, B, u = st["kind"], st["base"], st["u"]
                b = B.get

                if kind in ("norm", "init"):
                    if kind == "init":
                        pe.wait_ge(sem("x_loaded"), 16)
                        pe.wait_ge(sem("gains_ready"), 2)
                    for t in range(NT):
                        for half, name in ((0, "xn_act"), (1, "xn_dve")):
                            if kind == "norm":
                                pe.wait_ge(sem(name), b(name, 0) + t + 1)
                            for k in range(4 * half, 4 * half + 4):
                                last = pe.transpose(tb[:, k, t * P:(t + 1) * P], xn[:, t, k * P:(k + 1) * P], ident[:, :])
                            last.then_inc(sem("t_done"), 1)
                elif kind not in ("ffn", "final", "lift") and b("xl_ready", 0):
                    pe.wait_ge(sem("xl_ready"), b("xl_ready", 0))

                if kind == "ffn":
                    s0, s1, s2 = (u % 3, (u + 1) % 3, (u + 2) % 3)

                    def up(d, i):
                        unit_ready(pe, d, u)
                        if b("silu_done", 0) or not isinstance(i, int):
                            pe.wait_ge(sem("silu_done"), i + b("silu_done", 0))
                        feature_major(pe, ps[:, 4, 0:S], s0, 0, KT, 256, lows=b("xl_ready") - 4)
                        used(feature_major(pe, ps[:, 4, S:], s0, P, KT, 256))
                        unit_ready(pe, d, u + 1)
                        if b("g_made", 0) or not isinstance(i, int):
                            pe.wait_ge(sem("g_made"), i * 2 + b("g_made", 0))
                        feature_major(pe, ps[:, 5, 0:S], s1, 0, KT, 256).then_inc(sem("up0_done"), 1)
                        used(feature_major(pe, ps[:, 6, 0:S], s1, P, KT, 256))

                    def dn(d, i):
                        unit_ready(pe, d, u + 2)
                        for c in range(2):
                            pe.wait_ge(sem("gl_ready"), i * 2 + (b("gl_ready", 0) + c + 1))
                            for t in range(NT):
                                for n in range(2):
                                    c0 = c * DM + n * 512
                                    last = mm3(pe, y[:, t, n, :], oh[:, c, t * P:(t + 1) * P], ol[:, c, t * P:(t + 1) * P],
                                               whi[:, s2, c0:c0 + 512], wlo[:, s2, c0:c0 + 512], False, False)
                        used(last)

                    up(0, 0)
                    residual(pe, dict(base=dict(cx_ready=b("cx_ready", 0))))
                    with pe.Fori(0, FIT - 1) as i:
                        dn((i, 3), i)
                        up2 = (i, 3)
                        unit_ready(pe, up2, u + 3)
                        pe.wait_ge(sem("silu_done"), i + (b("silu_done", 0) + 1))
                        feature_major(pe, ps[:, 4, 0:S], s0, 0, KT, 256)
                        used(feature_major(pe, ps[:, 4, S:], s0, P, KT, 256))
                        unit_ready(pe, up2, u + 4)
                        pe.wait_ge(sem("g_made"), i * 2 + (b("g_made", 0) + 2))
                        feature_major(pe, ps[:, 5, 0:S], s1, 0, KT, 256).then_inc(sem("up0_done"), 1)
                        used(feature_major(pe, ps[:, 6, 0:S], s1, P, KT, 256))
                    dn(3 * (FIT - 1), FIT - 1)

                if kind == "index":
                    n = st["j"]
                    for m in range(3):
                        unit_ready(pe, 0, u + m)
                        for t in range(NT):
                            w = 256 if m < 2 else 72
                            last = token_major(pe, ps[:, m, t * w:t * w + w], (u + m) % 3, 0, w, t, range(KT), w)
                        used(last)
                    pe.wait_ge(sem("ix_roped"), n + 1)
                    kid = qk_tm[:, 1024:1280].rearrange("p (t c) -> p t c", t=NT)
                    for m in range(4):
                        for t in range(NT):
                            src = qk_tm[:, (m // 2) * 512 + t * 256 + (m % 2) * P:][:, 0:P]
                            last = pe.transpose(ps[:, 5 + m // 2, (m % 2) * S + t * P:][:, 0:P], src, ident[:, :])
                        if m % 2:
                            last.then_inc(sem("ix_t"), 1)
                    for t in range(NT):
                        last = pe.transpose(ps[:, 7, t * P:(t + 1) * P], kid[:, t, :], ident[:, :])
                    last.then_inc(sem("ix_t"), 1)
                    pe.wait_ge(sem("ix_k"), n + 1)
                    for h in range(8):
                        if h == 4:
                            pe.wait_ge(sem("ix_q1"), n + 1)
                        if h >= 2:
                            pe.wait_ge(sem("ix_relu"), 8 * n + h - 1)
                        r0 = DH * (h % 2)
                        qT = qkT[r0:r0 + DH, h // 4, ((h // 2) % 2) * S:][:, 0:S]
                        kT = qkT[r0:r0 + DH, 2, 0:S]
                        o = ps[:, 3 + h % 2, :]
                        pe.matmul(o[:, 0:P], qT[:, 0:P], kT[:, 0:P], start=True, stop=True)
                        pe.matmul(o[:, P:3 * P], qT[:, P:S], kT, start=True, stop=True).then_inc(sem("ix_dots"), 1)

                if kind == "forget":
                    unit_ready(pe, 0, u)
                    for t in range(NT):
                        last = token_major(pe, ps[:, 0, t * 16:t * 16 + 16], u % 3, 0, 16, t, range(KT), 16)
                    used(last)
                    pe.wait_ge(sem("fg_lf"), 1)
                    for t in range(NT):
                        last = pe.matmul(ps[0:16, 7, 0:S], zf[:, 2, t, :], upper[:, t, :], start=t == 0, stop=t == 1)
                    last.then_inc(sem("fg_cum"), 1)

                if kind == "latent":
                    for m, ks in enumerate((range(0, 3), range(3, 6), range(6, 8))):
                        unit_ready(pe, 0, u + m)
                        for t in range(NT):
                            for bk, c0, n in ((t, 0, QL), (2 + t, QL, KVL + RP)):
                                last = token_major(pe, ps[:, bk, 0:n], (u + m) % 3, c0, n, t, ks, MLA_IN,
                                                   first=m == 0, final=m == 2, row0=ks[0])
                        used(last)
                    pe.wait_ge(sem("la_cn"), 2)
                    for k in range(5):
                        for t in range(NT):
                            last = pe.transpose(ps[:, 5 + k // 2, (k % 2) * S + t * P:][:, 0:P],
                                                xn[:, t, k * P:(k + 1) * P], ident[:, :])
                    last.then_inc(sem("la_t"), 1)
                    pe.wait_ge(sem("la_cl"), 1)

                if kind == "attn":
                    mla = st["mix"] == "mla"
                    R = 8 if mla else 6
                    D = MD if mla else DH
                    pt0 = 4 if mla else 2
                    moved = 3 if mla else 2
                    tm = qk_tm[:, 0:2 * NT * 4 * D].rearrange("p (a t h d) -> p a t h d", a=2, t=NT, h=4)

                    def proj(q, j, d, u0):
                        slot = u0 % 3
                        unit_ready(pe, d, u0)
                        first = isinstance(q, int) and q == 0
                        if "col" not in st and not first:
                            if mla and j:
                                pe.wait_ge(sem("qk_moved"), q * 3 + (b("qk_moved", 0) - 3 + (3 if j == 1 else 5)))
                                pe.wait_ge(sem("kv_moved"), q * 2 + (j - 1))
                            elif j < 2:
                                pe.wait_ge(sem("qk_moved"), q * moved + (b("qk_moved", 0) - moved + j + 1))
                            else:
                                pe.wait_ge(sem("v_moved"), q + b("v_moved", 0))
                        elif mla and j == 2:
                            pe.wait_ge(sem("qk_moved"), b("qk_moved", 0) + 2)
                            pe.wait_ge(sem("kv_moved"), 1)
                        for t in range(NT):
                            if mla and j == 0:
                                last = token_major(pe, ps[:, t, 0:384], slot, 0, 384, t, range(3), 384)
                            elif mla:
                                last = token_major(pe, ps[:, 2, t * 256:(t + 1) * 256], slot, 0, 256, t, range(2), 256, k0=3)
                            else:
                                last = token_major(pe, ps[:, j, t * 256:(t + 1) * 256], slot, 0, 256, t, range(KT), 256)
                        used(last)

                    def x_free(q, r):
                        half = R // 2
                        name = f"x_moved{r % 2}"
                        v = b(name, 0) + r // 2
                        pe.wait_ge(sem(name), q * half + v)

                    def turn(q, m):
                        for k in range(2 if mla else 1):
                            r = 2 * m + k if mla else m
                            x_free(q, r)
                            for n, (aq, t) in enumerate(((0, 0), (0, 1), (1, 0), (1, 1))):
                                if "col" in st:
                                    if aq == 0:
                                        src = qk_tm[:, 512 * q + 256 * t + P * m:512 * q + 256 * t + P * m + P]
                                    else:
                                        src = kd[:, t, q, :, :].rearrange("p n d -> p (n d)")
                                    last = pe.transpose(ps[:, 5 + r % 2, n * P:(n + 1) * P], src, ident[:, :])
                                elif mla:
                                    last = pe.transpose(ps[0:MD, 5 + r % 2, n * P:(n + 1) * P], tm[:, aq, t, r, :], ident[:, :])
                                else:
                                    src = tm[:, aq, t, 2 * m:2 * m + 2, :].rearrange("p h d -> p (h d)")
                                    last = pe.transpose(ps[:, 5 + r % 2, n * P:(n + 1) * P], src, ident[:, :])
                            last.then_inc(sem("x_filled"), 1)

                    def scores(q, h):
                        if mla:
                            pe.wait_ge(sem(f"x_moved{h % 2}"), q * (R // 2) + (b(f"x_moved{h % 2}", 0) + h // 2 + 1))
                            A = qkT[0:MD, h, :]
                        else:
                            pe.wait_ge(sem(f"x_moved{h // 2}"), q * (R // 2) + (b(f"x_moved{h // 2}", 0) + 1))
                            A = qkT[DH * (h % 2):DH * (h % 2) + DH, h // 2, :]
                        if b("masked", 0) or h >= 2:
                            pe.wait_ge(sem("masked"), q * 4 + (b("masked", 0) + h - 1))
                        o = ps[:, 3 + h % 2, :]
                        fox = st["mix"] == "fox"
                        for c0, c1, qa, ka in ((0, P, A[:, 0:P], A[:, S:S + P]), (P, 3 * P, A[:, P:S], A[:, S:])):
                            last = pe.matmul(o[:, c0:c1], qa, ka, start=True, stop=not fox)
                            if fox:
                                row = selcum[:, bass.ds(q * 4 + h, 1), 0:c1 - c0].rearrange("p a s -> p (a s)")
                                last = pe.matmul(o[:, c0:c1], ones[0:16, :], row, start=False, stop=True)
                        last.then_inc(sem("s_filled"), 1)

                    def pturn(q, h):
                        x_free(q, pt0 + h)
                        pe.wait_ge(sem("p_ready"), q * 4 + (b("p_ready", 0) + h + 1))
                        for n in range(3):
                            last = pe.transpose(ps[:, 5 + h % 2, n * P:(n + 1) * P], pr[:, h % 2, n * P:(n + 1) * P], ident[:, :])
                        last.then_inc(sem("x_filled"), 1)

                    def values(q, h):
                        pe.wait_ge(sem(f"x_moved{h % 2}"), q * (R // 2) + (b(f"x_moved{h % 2}", 0) + (pt0 + h) // 2 + 1))
                        if h == 0:
                            if "col" in st:
                                pe.wait_ge(sem("v_moved"), b("v_moved") + 1)
                            elif mla:
                                pe.wait_ge(sem("mla_v"), q + 1)
                            else:
                                pe.wait_ge(sem("v_moved"), q + (b("v_moved", 0) + 1))
                        if h % 2 == 0:
                            v = b("ol_ready", 0) + h // 2
                            if v or not isinstance(q, int):
                                pe.wait_ge(sem("ol_ready"), q * 2 + v)
                        r0, m = DH * (h % 2), h // 2
                        o = ps[r0:r0 + DH, 7, 0:S]
                        pt = pT[:, h % 2, :]
                        vh = q if "col" in st else h
                        pe.matmul(o[:, 0:P], v_tm[:, 0, vh, :], pt[:, 0:P], start=True, stop=True)
                        pe.matmul(o[:, P:], v_tm[:, 0, vh, :], pt[:, P:2 * P], start=True, stop=False)
                        pe.matmul(o[:, P:], v_tm[:, 1, vh, :], pt[:, 2 * P:], start=False, stop=True).then_inc(sem("av_done"), 1)

                    def quad(q, nxt):
                        if "col" in st:
                            pe.wait_ge(sem("qk_moved"), b("qk_moved", 0) + 4)
                        elif st["mix"] == "fox":
                            pe.wait_ge(sem("qk_moved"), q * 2 + (b("qk_moved", 0) + 2))
                        else:
                            pe.wait_ge(sem("rope_done"), q + (b("rope_done") + 1))
                        if mla:
                            pe.wait_ge(sem("qk_moved"), q * 3 + (b("qk_moved", 0) + 3))
                        d = (q, 3)
                        turn(q, 0)
                        if nxt:
                            proj(q + 1, 0, d, u + 3)
                        scores(q, 0)
                        scores(q, 1)
                        turn(q, 1)
                        if nxt:
                            proj(q + 1, 1, d, u + 4)
                        pturn(q, 0)
                        pturn(q, 1)
                        scores(q, 2)
                        scores(q, 3)
                        values(q, 0)
                        values(q, 1)
                        if nxt:
                            proj(q + 1, 2, d, u + 5)
                        pturn(q, 2)
                        pturn(q, 3)
                        values(q, 2)
                        values(q, 3)

                    for j in range(3):
                        proj(0, j, 0, u + j)
                    if "col" in st:
                        for q in range(NQ2):
                            quad(q, False)
                        continue
                    if st["mix"] == "fox":
                        pe.wait_ge(sem("fg_sel"), 1)
                    if mla:
                        pe.wait_ge(sem("la_krope"), 1)
                    with pe.Fori(0, NG - 1) as q:
                        quad(q, True)
                    quad(NG - 1, False)

                if kind in ("oproj", "oproj2"):
                    if kind == "oproj2":
                        pe.wait_ge(sem("gate_used"), 12)
                    residual(pe, dict(base=dict(cx_ready=b("cx_ready", 0))))
                    src = (oh, ol) if kind == "oproj" else (xh, xl)
                    if kind == "oproj":
                        pe.wait_ge(sem("ol_ready"), b("ol_ready", 0))
                    else:
                        pe.wait_ge(sem("mix_lo"), 4)
                    for m in range(4):
                        unit_ready(pe, 0, u + m)
                        slot = (u + m) % 3
                        for c in range(2):
                            for t in range(NT):
                                for n in range(2):
                                    k, c0 = 2 * m + c, c * DM + n * 512
                                    last = mm3(pe, y[:, t, n, :], src[0][:, k, t * P:(t + 1) * P], src[1][:, k, t * P:(t + 1) * P],
                                               whi[:, slot, c0:c0 + 512], wlo[:, slot, c0:c0 + 512], False, False)
                        used(last)

                if kind == "lift":
                    residual(pe, dict(base=dict(cx_ready=b("cx_ready"))))
                    pe.drain().then_inc(sem("lift_done"), 1)

                if kind == "ssm_in":
                    for m in range(2):
                        unit_ready(pe, 0, u + m)
                        feature_major(pe, ps[:, m, 0:S], (u + m) % 3, 0, KT, 256)
                        used(feature_major(pe, ps[:, m, S:], (u + m) % 3, P, KT, 256))

                if kind == "ssm":
                    def blocks(q):
                        pe.wait_ge(sem("z_built"), q + 1)
                        if q:
                            pe.wait_ge(sem("bt_moved"), q)
                            pe.wait_ge(sem("cl_built"), q)
                        for j in range(4):
                            for r in range(2):
                                n = 2 * j + r
                                pe.transpose(ps[:, n // 4, (n % 4) * P:(n % 4 + 1) * P], Z[:, j, r, :], ident[:, :])
                        for r in range(2):
                            last = pe.transpose(ps[0:64, 2, r * P:(r + 1) * P], cc[:, q, r, :], ident[:, :])
                        last.then_inc(sem("bt_turned"), 1)

                    def inputs(n):
                        pe.wait_ge(sem("bt_moved"), n // 4 + 1)
                        if n >= 2:
                            pe.wait_ge(sem("w_made"), n - 1)
                        for r in range(2):
                            last = pe.matmul(ps[:, 3 + n % 2, r * S:(r + 1) * S], BT[:, 2 * (n % 4) + r, :], uT[:, n // 4, :],
                                             start=True, stop=True)
                        last.then_inc(sem("x_made"), 1)

                    def outputs(n):
                        q = n // 4
                        if n % 4 == 0:
                            pe.wait_ge(sem("cl_built"), q + 1)
                            if q >= 2:
                                pe.wait_ge(sem("ys_made"), q - 1)
                        pe.wait_ge(sem("h_made"), n + 1)
                        for r in range(2):
                            last = pe.matmul(ps[:, 5 + q % 2, 0:S], CL[:, n % 4, r, :], hv[n % 2][:, r, :],
                                             start=n % 4 == 0 and r == 0, stop=n % 4 == 3 and r == 1)
                        last.then_inc(sem("y_used"), 1)

                    blocks(0)
                    inputs(0)
                    for n in range(16):
                        if n < 15:
                            if n % 4 == 3:
                                blocks(n // 4 + 1)
                            inputs(n + 1)
                        outputs(n)

                if kind == "glu":
                    pe.wait_ge(sem("gel_lo"), 4)
                    for m in range(2):
                        unit_ready(pe, 0, u + m)
                        for f in range(4):
                            last = feature_major(pe, ps[:, 2 * m + f // 2, (f % 2) * S:(f % 2 + 1) * S], (u + m) % 3, f * P, 4, 512, h=bh, l=bl)
                        used(last)
                    pe.drain().then_inc(sem("glu_done"), 1)

                if kind == "branches":
                    for J in range(2):
                        for m, (h, l) in enumerate(((oh[:, 0:4, :], ol[:, 0:4, :]), (bh, bl), (oh[:, 4:8, :], ol[:, 4:8, :]))):
                            v = u + 9 * J + m
                            unit_ready(pe, 0, v)
                            if m == 0:
                                pe.wait_ge(sem("glu_lo"), 2)
                                if J:
                                    pe.wait_ge(sem("gate_used"), 6)
                            for f in range(4):
                                last = feature_major(pe, ps[:, 2 * m + f // 2, (f % 2) * S:(f % 2 + 1) * S], v % 3, f * P, 4, 512, h=h, l=l)
                            used(last)
                        for g in range(6 * J, 6 * J + 6):
                            v = u + 3 * J + g + 3
                            unit_ready(pe, 0, v)
                            if g >= 2:
                                pe.wait_ge(sem("gate_sig"), g - 1)
                            feature_major(pe, ps[:, 6 + g % 2, 0:S], v % 3, 0, KT, 256)
                            used(feature_major(pe, ps[:, 6 + g % 2, S:], v % 3, P, KT, 256))

                if kind == "ff":
                    def up(i, j, k0, v, d):
                        unit_ready(pe, d, v)
                        if k0 >= 3:
                            pe.wait_ge(sem("relu_done"), i * 3 + (k0 - 2))
                        feature_major(pe, ps[:, 4 + j, 0:S], v % 3, 0, KT, 256)
                        used(feature_major(pe, ps[:, 4 + j, S:], v % 3, P, KT, 256))

                    def dn2(i, j, k0, v, d):
                        unit_ready(pe, d, v)
                        pe.wait_ge(sem("fl_ready"), i * 3 + (k0 + 1))
                        for c in range(2):
                            for t in range(NT):
                                for n in range(2):
                                    c0 = c * DM + n * 512
                                    last = mm3(pe, y[:, t, n, :], oh[:, 2 * j + c, t * P:(t + 1) * P], ol[:, 2 * j + c, t * P:(t + 1) * P],
                                               whi[:, v % 3, c0:c0 + 512], wlo[:, v % 3, c0:c0 + 512], False, False)
                        used(last)

                    def turn(i, j, k0, d):
                        up(i, (j + 1) % 3, k0 + 1, u + 1 + 2 * k0, d)
                        dn2(i, j, k0, u + 2 + 2 * k0, d)

                    up(0, 0, 0, u, 0)
                    for t in range(NT):
                        for n in range(2):
                            pe.matmul(y[:, t, n, :], ident[:, :], x2[:, t, n * 512:(n + 1) * 512], start=True, stop=False,
                                      skip_group_check=True)
                    for k0 in range(3):
                        turn(0, k0, k0, 0)
                    with pe.Fori(0, 3) as i:
                        for j in range(3):
                            turn(i, j, 3 + j, (i, 6))
                    for k0 in (12, 13, 14):
                        turn(0, k0 % 3, k0, 0)
                    dn2(0, 0, 15, u + 31, 0)


_INS = ["x", "ffn1_w13", "ffn1_w2", "ffn2_w13", "ffn2_w2", "ln_g", "ln_b", "w_out", "dsa_w_in", "fox_w_in", "fox_b_f",
        "mla_w_dqkv", "mla_q_norm_g", "mla_w_uq", "mla_kv_norm_g", "mla_w_ukv", "norm_mix_2", "w_in_2", "sinks_2",
        "lam_re_2", "lam_im_2", "log_step_2", "b_re_2", "b_im_2", "c_re_2", "c_im_2", "d_skip_2", "w_glu_2",
        "w_o_swa_2", "w_o_ssm_2", "w_o_moba_2", "w_out_2", "norm_ffn_2", "w_ff1_2", "w_ff2_2", "norm_final_2"]
_OUTS = [((1, S, DM), "float32")]


def kernel(**inputs):
    import numpy as _np
    import concourse.bacc as _bacc
    from concourse import mybir as _mybir
    from concourse.bass_utils import run_bass_kernel_spmd as _run

    nc = _bacc.Bacc("TRN2", target_bir_lowering=False, num_devices=1)
    arrays, args = {}, {}
    for name in _INS:
        v = _np.ascontiguousarray(inputs[name])
        arrays[f"in_{name}_dram"] = v
        args[name] = nc.dram_tensor(f"in_{name}_dram", v.shape, _mybir.dt.from_np(v.dtype), kind="ExternalInput").ap()
    out = nc.dram_tensor("out_0_dram", _OUTS[0][0], _mybir.dt.float32, kind="ExternalOutput").ap()
    plan, n_units = stages_plan()
    build(nc, args, out, plan, n_units)
    r = _run(nc, [arrays], core_ids=[0])
    return r.results[0]["out_0_dram"]
```
